# Optimizing a Trainium2 kernel written in Bass

```python
import jax, jax.numpy as jnp
from jax import lax
import numpy as np

D_MODEL = 1024
BATCH = 1
SEQ = 1024
DEPTH = 2
DEC_BATCH = 8
DEC_SEQ = 8
PAST_LEN = 4096
PAGE_SIZE = 128

N_A = DEPTH // 2
N_B = DEPTH - N_A
CONV_W = 31
E_A = 2 * D_MODEL
HEAD_DIM = 64
N_HEADS = D_MODEL // HEAD_DIM
E_B = N_HEADS * HEAD_DIM
PLE_DIM = 256
Q_BLOCK = 128
F_BIAS_INIT = 3.0
EPS = 1e-6

kernel_name = 'yoco_conformer_fox_decode_step'

def rms_norm(x, g):
    x32 = x.astype(jnp.float32)
    y = x32 * lax.rsqrt(jnp.mean(x32 * x32, axis=-1, keepdims=True) + EPS)
    return y.astype(x.dtype) * g

def layer_norm(x, g, b):
    x32 = x.astype(jnp.float32)
    mu = jnp.mean(x32, axis=-1, keepdims=True)
    xc = x32 - mu
    y = xc * lax.rsqrt(jnp.mean(xc * xc, axis=-1, keepdims=True) + EPS)
    return y.astype(x.dtype) * g + b

def conv_mixer(x, prev, norm_g, w_in, conv_w, conv_b, ln_g, ln_b, w_out):
    h = rms_norm(x, norm_g)
    a, b, z = jnp.split(h @ w_in, 3, axis=-1)
    u = a * jax.nn.sigmoid(b)
    u_ext = jnp.concatenate([prev.astype(u.dtype), u], axis=1)
    c = lax.conv_general_dilated(u_ext, conv_w[:, None, :], window_strides=(1,), padding='VALID',
                                 dimension_numbers=('NWC', 'WIO', 'NWC'),
                                 feature_group_count=E_A) + conv_b
    c = jax.nn.silu(layer_norm(c, ln_g, ln_b))
    out = (c * jax.nn.silu(z)) @ w_out
    return out, u_ext[:, -(CONV_W - 1):]

def shared_kv(x, kv_norm, kv_w, k_norm, f_bias):
    bsz, s = x.shape[:2]
    h = rms_norm(x, kv_norm)
    proj = h @ kv_w
    k = proj[..., :E_B].reshape(bsz, s, N_HEADS, HEAD_DIM)
    v = proj[..., E_B:2 * E_B].reshape(bsz, s, N_HEADS, HEAD_DIM)
    fl = proj[..., 2 * E_B:] + f_bias
    k = rms_norm(k, k_norm)
    logf = jax.nn.log_sigmoid(fl.astype(jnp.float32))
    return k, v, logf

def fox_attend(q, k, v, cq, ck, q_pos, k_pos):
    s = jnp.einsum('bqhd,bkhd->bhqk', q, k).astype(jnp.float32) * (HEAD_DIM ** -0.5)
    s = s + (jnp.transpose(cq, (0, 2, 1))[..., :, None] - jnp.transpose(ck, (0, 2, 1))[..., None, :])
    mask = k_pos[None, :] <= q_pos[:, None]
    s = jnp.where(mask, s, jnp.finfo(jnp.float32).min)
    p = jax.nn.softmax(s, axis=-1).astype(v.dtype)
    return jnp.einsum('bhqk,bkhd->bqhd', p, v)

def fox_prompt(q, k, v, c):
    bsz, s = q.shape[:2]
    n_blocks = s // Q_BLOCK
    k_pos = jnp.arange(s, dtype=jnp.int32)

    def block(i):
        st = i * Q_BLOCK
        qb = lax.dynamic_slice_in_dim(q, st, Q_BLOCK, axis=1)
        cb = lax.dynamic_slice_in_dim(c, st, Q_BLOCK, axis=1)
        qp = st + jnp.arange(Q_BLOCK, dtype=jnp.int32)
        return fox_attend(qb, k, v, cb, c, qp, k_pos)

    out = lax.map(block, jnp.arange(n_blocks, dtype=jnp.int32))
    return jnp.transpose(out, (1, 0, 2, 3, 4)).reshape(bsz, s, N_HEADS, HEAD_DIM)

def fox_layer(x, attend, norm_g, w_q, q_norm, w_out):
    bsz, s = x.shape[:2]
    h = rms_norm(x, norm_g)
    qz = h @ w_q
    q = rms_norm(qz[..., :E_B].reshape(bsz, s, N_HEADS, HEAD_DIM), q_norm)
    z = qz[..., E_B:]
    o = attend(q).reshape(bsz, s, E_B)
    return (o * jax.nn.silu(z)) @ w_out

def run_group(x, p, conv_prev, past_k, past_v, past_logf,
              a_norm, a_w_in, a_conv_w, a_conv_b, a_ln_g, a_ln_b, a_w_out,
              kv_norm, kv_w, kv_k_norm, kv_f_bias,
              b_norm, b_w_q, b_q_norm, b_w_out, ple_w, ple_gate_w):
    t = x.shape[1]
    conv_states = []
    k_new = v_new = logf_new = None
    attend = None
    for i in range(DEPTH):
        if i < N_A:
            o, st = conv_mixer(x, conv_prev[i], a_norm[i], a_w_in[i], a_conv_w[i], a_conv_b[i],
                               a_ln_g[i], a_ln_b[i], a_w_out[i])
            conv_states.append(st)
        else:
            if i == N_A:
                k_new, v_new, logf_new = shared_kv(x, kv_norm, kv_w, kv_k_norm, kv_f_bias)
                if past_k is None:
                    c_all = jnp.cumsum(logf_new, axis=1)
                    attend = lambda q, k=k_new, v=v_new, c=c_all: fox_prompt(q, k, v, c)
                else:
                    p_len = past_k.shape[1]
                    k_all = jnp.concatenate([past_k.astype(k_new.dtype), k_new], axis=1)
                    v_all = jnp.concatenate([past_v.astype(v_new.dtype), v_new], axis=1)
                    c_all = jnp.cumsum(jnp.concatenate([past_logf.astype(jnp.float32), logf_new], axis=1), axis=1)
                    q_pos = p_len + jnp.arange(t, dtype=jnp.int32)
                    k_pos = jnp.arange(p_len + t, dtype=jnp.int32)
                    attend = lambda q, k=k_all, v=v_all, c=c_all, qp=q_pos, kp=k_pos, pl=p_len: fox_attend(q, k, v, c[:, pl:], c, qp, kp)
            j = i - N_A
            o = fox_layer(x, attend, b_norm[j], b_w_q[j], b_q_norm[j], b_w_out[j])
        x = x + o
        x = x + jax.nn.sigmoid(x @ ple_gate_w[i]) * (p[i].astype(x.dtype) @ ple_w[i])
    return x, jnp.stack(conv_states, axis=0), k_new, v_new, logf_new

def setup_inputs(seed: int = 0) -> dict:
    key = jax.random.key(seed)
    ks = jax.random.split(key, 32)
    n_pages = PAST_LEN // PAGE_SIZE
    n_used = DEC_BATCH * n_pages
    n_pool = n_used + max(1, n_used // 4)
    f32 = jnp.float32

    def nrm(k, shape, scale):
        return jax.random.normal(k, shape, f32) * scale

    perm = jax.random.permutation(ks[0], n_pool)
    page_table = perm[:n_used].reshape(DEC_BATCH, n_pages).astype(jnp.int32)
    return {
        'x_prompt': nrm(ks[1], (BATCH, SEQ, D_MODEL), 1.0),
        'x_sample': nrm(ks[2], (DEC_BATCH, DEC_SEQ, D_MODEL), 1.0),
        'state_conv': nrm(ks[3], (N_A, DEC_BATCH, CONV_W - 1, E_A), 1.0),
        'cache_k': nrm(ks[4], (n_pool, PAGE_SIZE, N_HEADS, HEAD_DIM), 1.0),
        'cache_v': nrm(ks[5], (n_pool, PAGE_SIZE, N_HEADS, HEAD_DIM), 1.0),
        'cache_logf': jax.nn.log_sigmoid(F_BIAS_INIT + nrm(ks[6], (n_pool, PAGE_SIZE, N_HEADS), 1.0)),
        'page_table': page_table,
        'p_prompt': nrm(ks[7], (DEPTH, BATCH, SEQ, PLE_DIM), 1.0),
        'p_sample': nrm(ks[8], (DEPTH, DEC_BATCH, DEC_SEQ, PLE_DIM), 1.0),
        'a_norm': 1.0 + nrm(ks[9], (N_A, D_MODEL), 0.02),
        'a_w_in': nrm(ks[10], (N_A, D_MODEL, 3 * E_A), D_MODEL ** -0.5),
        'a_conv_w': nrm(ks[11], (N_A, CONV_W, E_A), CONV_W ** -0.5),
        'a_conv_b': nrm(ks[12], (N_A, E_A), 0.02),
        'a_ln_g': 1.0 + nrm(ks[13], (N_A, E_A), 0.02),
        'a_ln_b': nrm(ks[14], (N_A, E_A), 0.02),
        'a_w_out': nrm(ks[15], (N_A, E_A, D_MODEL), E_A ** -0.5),
        'kv_norm': 1.0 + nrm(ks[16], (D_MODEL,), 0.02),
        'kv_w': nrm(ks[17], (D_MODEL, 2 * E_B + N_HEADS), D_MODEL ** -0.5),
        'kv_k_norm': 1.0 + nrm(ks[18], (HEAD_DIM,), 0.02),
        'kv_f_bias': F_BIAS_INIT + nrm(ks[19], (N_HEADS,), 0.1),
        'b_norm': 1.0 + nrm(ks[20], (N_B, D_MODEL), 0.02),
        'b_w_q': nrm(ks[21], (N_B, D_MODEL, 2 * E_B), D_MODEL ** -0.5),
        'b_q_norm': 1.0 + nrm(ks[22], (N_B, HEAD_DIM), 0.02),
        'b_w_out': nrm(ks[23], (N_B, E_B, D_MODEL), E_B ** -0.5),
        'ple_w': nrm(ks[24], (DEPTH, PLE_DIM, D_MODEL), PLE_DIM ** -0.5),
        'ple_gate_w': nrm(ks[25], (DEPTH, D_MODEL, D_MODEL), D_MODEL ** -0.5),
    }

def reference(x_prompt, x_sample, state_conv, cache_k, cache_v, cache_logf, page_table,
              p_prompt, p_sample,
              a_norm, a_w_in, a_conv_w, a_conv_b, a_ln_g, a_ln_b, a_w_out,
              kv_norm, kv_w, kv_k_norm, kv_f_bias,
              b_norm, b_w_q, b_q_norm, b_w_out, ple_w, ple_gate_w):
    db, n_pages = page_table.shape

    def gather(pool):
        g = pool[page_table]
        return g.reshape((db, n_pages * pool.shape[1]) + pool.shape[2:])

    conv0 = jnp.zeros((N_A, x_prompt.shape[0], CONV_W - 1, E_A), x_prompt.dtype)
    y_prompt, conv_p, k_p, v_p, lf_p = run_group(
        x_prompt, p_prompt, conv0, None, None, None,
        a_norm, a_w_in, a_conv_w, a_conv_b, a_ln_g, a_ln_b, a_w_out,
        kv_norm, kv_w, kv_k_norm, kv_f_bias,
        b_norm, b_w_q, b_q_norm, b_w_out, ple_w, ple_gate_w)
    y_sample, conv_s, k_s, v_s, lf_s = run_group(
        x_sample, p_sample, state_conv, gather(cache_k), gather(cache_v), gather(cache_logf),
        a_norm, a_w_in, a_conv_w, a_conv_b, a_ln_g, a_ln_b, a_w_out,
        kv_norm, kv_w, kv_k_norm, kv_f_bias,
        b_norm, b_w_q, b_q_norm, b_w_out, ple_w, ple_gate_w)
    return (y_prompt, y_sample, conv_p, k_p, v_p, lf_p, conv_s, k_s, v_s, lf_s)


_drawn_inputs = setup_inputs


def setup_inputs(seed=0):
    import zlib

    import numpy as np

    out = dict(_drawn_inputs(seed))
    spreads = {}
    factors = {'cache_logf': 3.185,
     'a_conv_b': 4.768,
     'a_ln_g': 7.443,
     'a_ln_b': 8.0,
     'kv_norm': 2.84,
     'kv_k_norm': 2.833,
     'b_norm': 8.0,
     'b_q_norm': 8.0}
    for name, (base, spread) in spreads.items():
        noise = np.random.default_rng([zlib.crc32(name.encode()), seed]).standard_normal(out[name].shape)
        drawn = base * np.exp(spread * noise) if base else spread * noise
        out[name] = __import__('jax').numpy.asarray(drawn.astype(out[name].dtype))
    for name, factor in factors.items():
        out[name] = (out[name] * factor).astype(out[name].dtype)
    return out
```

```python
from contextlib import ExitStack

import concourse.bass as bass
from concourse import mybir

F32 = mybir.dt.float32
F32R = mybir.dt.float32r
BF16 = mybir.dt.bfloat16
I32 = mybir.dt.int32
ALU = mybir.AluOpType
ACT = mybir.ActivationFunctionType
AX_X = mybir.AxisListType.X
ds = bass.ds

P = 128
D = 1024
KD = D // P
SEQ = 1024
DB, DS = 8, 8
RS = DB * DS
R = SEQ + RS
RCH = [(0, 384), (384, 768), (768, R)]
EA = 2 * D
NCH = EA // P
CW = 31
HIST = CW - 1
H, HD = 16, 64
PAIRS = H // 2
PLE = 256
EPS = 1e-6
PAST, PAGE = 4096, 128
NPG = PAST // PAGE
GP = 4
NG = NPG // GP
NQ = SEQ // P
USAMP = HIST + SEQ
SW = HIST + DS
UEXT = USAMP + DB * SW
NT = 9
NV = CW - NT
SLOT = 10 * P
U_CONV, U_OUT, U_PLE, U_K, U_V, U_F, U_Q, U_Z, U_TAIL = 0, 48, 64, 72, 80, 88, 89, 97, 105
F_STEPS = 22
C_AN, C_KN, C_BN, C_LG, C_LB, C_K2, C_Q2, C_FB, C_EPS, C_EPQ, C_N = 0, 8, 16, 24, 40, 56, 57, 58, 59, 60, 61
B_ID, B_MD, B_SD, B_SP, B_MN, B_BF, B_M4, B_N = 0, 128, 256, 384, 640, 1152, 1152, 1408
TILE = 4352


def atleast(eng, sem, value):
    if not isinstance(value, int) or value > 0:
        eng.wait_ge(sem, value)


def flat(ap):
    return ap.rearrange("p a n -> p (a n)")


def build(nc, xT, pT, wA, wO, wP, wB, wW, cw, est, cst, fcon, bcon, ck, cv, clf, ptab,
          yT, cpT, csT, kT, vR, lfT):
    zT = nc.dram_tensor("zT_scr", (NCH, P, R), F32, kind="Internal").ap()
    qT = nc.dram_tensor("qT_scr", (PAIRS, P, R), F32, kind="Internal").ap()
    gT = nc.dram_tensor("gT_scr", (PAIRS, P, R), F32, kind="Internal").ap()
    lfG = nc.dram_tensor("lfG_scr", (DB * H, PAST), F32, kind="Internal").ap()
    cPr = nc.dram_tensor("cPr_scr", (3, H, SEQ), BF16, kind="Internal").ap()
    cPa = nc.dram_tensor("cPa_scr", (3, DB * H, PAST), BF16, kind="Internal").ap()
    cNw = nc.dram_tensor("cNw_scr", (3, H, RS), BF16, kind="Internal").ap()
    with ExitStack() as ctx:
        sbuf_base = (nc.sbuf_base + 31) // 32 * 32
        sbuf_end = nc.sbuf_usable_end

        class Map:
            def __init__(self, at):
                self.at = at

            def __call__(self, name, shape, dt=F32):
                n = 2 if dt == BF16 else 4
                for s in shape[1:]:
                    n *= s
                t = nc.alloc_sbuf_tensor_at(name, shape, dt, offset=self.at)
                self.at += (n + 31) // 32 * 32
                assert self.at <= sbuf_end, (name, self.at, sbuf_end)
                return t

        def sem(name):
            return ctx.enter_context(nc.semaphore(name))

        PS = ctx.enter_context(nc.psum_tensor("PS", [P, 8, 512], F32))

        m = Map(sbuf_base)
        CST = m("CST", [P, C_N])
        FCON = m("FCON", [P, 3, P])
        IDENT, ONES, BONES = FCON[:, 0, :], FCON[:, 1, :], FCON[:, 2, :]
        PTAB = m("PTAB", [1, DB * NPG], I32)
        at_x = m.at
        UX = [m(f"UX{s}", [P, UEXT]) for s in range(2)]
        ZS = m("ZS", [P, R])
        PROD = [m(f"PROD{s}", [P, R]) for s in range(2)]
        ACC = m("ACC", [P, R])
        CSUM = m("CSUM", [P, R])
        CHAIN = m("CHAIN", [P, R])
        CWT = [m(f"CWT{s}", [P, CW + 1]) for s in range(2)]
        at_h = m.at
        HH = m("HH", [P, KD, R], F32R)
        HL = m("HL", [P, KD, R], F32R)
        at_c = m.at
        CC = m("CC", [P, NCH, R])
        at_r = m.at
        RAW = [m(f"RAW{s}", [P, SLOT]) for s in range(2)]
        WH = [m(f"WH{s}", [P, SLOT], F32R) for s in range(2)]
        WL = [m(f"WL{s}", [P, SLOT], F32R) for s in range(2)]
        XIN = Map(at_c)("XIN", [P, KD, R])
        m = Map(at_x)
        T0 = [m(f"T0{s}", [P, R]) for s in range(2)]
        RSTD0 = m("RSTD0", [P, R])
        m = Map(at_x)
        MU = m("MU", [P, R])
        T1 = [m(f"T1{s}", [P, R]) for s in range(2)]
        Y1 = [m(f"Y1{s}", [P, R]) for s in range(2)]
        Z1 = [m(f"Z1{s}", [P, R]) for s in range(2)]
        MH = Map(at_h)("MH", [P, NCH, R], F32R)
        ML = Map(at_c)("ML", [P, NCH, R], F32R)
        X2 = Map(at_x)("X2", [P, KD, R])
        m = Map(at_h)
        XH = m("XH", [P, KD, R], F32R)
        XL = m("XL", [P, KD, R], F32R)
        m = Map(at_c)
        RSTD2 = m("RSTD2", [P, R])
        PR = m("PR", [P, 2, R])
        PH = m("PH", [P, 2, R], F32R)
        PL = m("PL", [P, 2, R], F32R)
        SG = m("SG", [P, R])
        T2 = m("T2", [P, R])
        SQ2 = m("SQ2", [P, R])
        SS2 = m("SS2", [P, R])
        m = Map(at_h)
        GH = m("GH", [P, KD, R], F32R)
        GL = m("GL", [P, KD, R], F32R)
        m = Map(at_c + TILE)
        KC = [m(f"KC{s}", [P, R]) for s in range(2)]
        SQ3 = m("SQ3", [P, R])
        RS3 = m("RS3", [P, R])
        KN = m("KN", [P, R])
        FL = m("FL", [P, R])
        LFP = m("LFP", [P, PAST])
        CUM = m("CUM", [P, 1 + PAST])
        PB = [m(f"PB{s}", [P, 3, 512], BF16) for s in range(2)]
        assert m.at <= at_r
        VR = Map(at_c + 3 * TILE)("VR", [P, R // P + 1, P])
        VRES = LFP
        FPB = Map(at_c + 3 * TILE)("FPB", [H, 3, R], BF16)

        m = Map(at_x + KD * R * 4)
        NMX = [m(f"NMX{s}", [P, 1]) for s in range(2)]
        MXP = [m(f"MXP{s}", [P, 1]) for s in range(2)]
        SMP = [m(f"SMP{s}", [P, 1]) for s in range(2)]
        RIP = [m(f"RIP{s}", [P, 1]) for s in range(2)]
        MXD = m("MXD", [P, NG + 1])
        SMD = m("SMD", [P, NG + 1])
        GMD, NGM, RID = m("GMD", [P, 1]), m("NGM", [P, 1]), m("RID", [P, 1])
        QD = m("QD", [P, PAIRS, 32])
        assert m.at <= at_h
        m = Map(at_h)
        KV = [m(f"KV{s}", [P, GP, D]) for s in range(4)]
        SC = m("SC", [P, PAST + P])
        CB = m("CB", [96, PAST + RS], BF16)
        KT = [m(f"KT{s}", [P, SEQ]) for s in range(2)]
        QT = [m(f"QT{s}", [P, SEQ]) for s in range(2)]
        CP = [m(f"CP{s}", [96, SEQ], BF16) for s in range(2)]
        VP = m("VP", [P, NQ, P])
        ZP = m("ZP", [P, SEQ])
        PP = [m(f"PP{s}", [P, SEQ]) for s in range(2)]
        PT = [m(f"PT{s}", [P, SEQ]) for s in range(2)]
        OP = [m(f"OP{s}", [P, SEQ]) for s in range(2)]
        WOP = [m(f"WOP{s}", [P, D]) for s in range(2)]
        PTD = [m(f"PTD{s}", [P, GP, P]) for s in range(2)]
        PTN = m("PTN", [RS, P])
        KNW = m("KNW", [P, PAIRS, RS])
        VNW = m("VNW", [RS, D])
        BCON = m("BCON", [P, B_BF], BF16)
        M4 = m("M4", [P, B_N - B_M4])
        OD = m("OD", [P, 4 * HD])
        OE = m("OE", [P, 2 * HD])
        OS = m("OS", [P, PAIRS, RS])
        BRAW = Map(at_h)("BRAW", [P, B_BF])
        m = Map(at_h)
        WOF = m("WOF", [P, PAIRS, D])
        ZSM = m("ZSM", [P, PAIRS, RS])
        YS = m("YS", [RS, D])

        s_con, s_pt = sem("con_in"), sem("ptab_in")
        s_xin = [sem(f"xin{k}") for k in range(KD)]
        s_raw = [sem(f"raw_in{s}") for s in range(2)]
        s_hi, s_lo, s_unit = sem("whi"), sem("wlo"), sem("unit_done")
        s_sq0, s_st0, s_sd0, s_rc0 = sem("sq0"), sem("stat0"), sem("sd0"), sem("rstd0")
        s_t0, s_hh, s_h = sem("h_f32"), sem("h_hi"), sem("h_lo")
        s_est = [sem(f"est_in{s}") for s in range(2)]
        s_pad, s_sg, s_u, s_zs, s_zst, s_cst = (sem(x) for x in ("pad", "sigb", "u", "zs", "z_out", "state_out"))
        s_prod, s_add, s_tap, s_c, s_csum = (sem(x) for x in ("prod", "add", "tap", "conv", "csum"))
        s_mmu, s_mu, s_xc, s_sq1, s_var, s_sd1, s_rc1 = (
            sem(x) for x in ("mu_mm", "mu", "xc", "sq1", "var_mm", "sd1", "rstd1"))
        s_t1, s_y1, s_m, s_mh, s_ml = (sem(x) for x in ("lnx", "lny", "m_f32", "m_hi", "m_lo"))
        s_z1 = [sem(f"z_in{s}") for s in range(2)]
        s_x1in, s_x1 = sem("x_in2"), sem("x1")
        s_xh, s_xl, s_prin, s_ph, s_pl = (sem(x) for x in ("x_hi", "x_lo", "p_in", "p_hi", "p_lo"))
        s_gate, s_sgp, s_t2, s_x2, s_sq2, s_ss2, s_st2, s_sd2, s_rc2 = (
            sem(x) for x in ("gate_mm", "gate_sig", "ple_prod", "x2", "sq2", "sumsq2", "stat2", "sd2", "rstd2"))
        s_g, s_gh, s_gl = sem("hkv_f32"), sem("hkv_hi"), sem("hkv_lo")
        s_kc, s_sq3, s_n, s_rs, s_rc, s_kn, s_kst = (
            sem(x) for x in ("kvq_copy", "sq3", "norm_mm", "norm_sd", "norm_rstd", "normed", "kq_out"))
        s_tr, s_vr, s_vst, s_zc = (sem(x) for x in ("v_transposed", "v_rows", "v_out", "z_silu"))
        s_gst = [sem(f"g_out{s}") for s in range(2)]
        s_fl, s_f, s_fe, s_fst = (sem(x) for x in ("fl", "logf_step", "logf_exp", "logf_out"))
        s_lfg, s_lfp, s_cum, s_pb, s_vres = (sem(x) for x in ("past_logf_gathered", "past_logf_in", "past_cum", "past_parts", "past_residual"))
        s_pst = [sem(f"past_out{s}") for s in range(2)]
        s_q, s_wo = [sem(f"kq_in{s}") for s in range(2)], [sem(f"wo_in{s}") for s in range(2)]
        s_kv = [sem(f"pages_in{s}") for s in range(4)]
        s_pad2, s_bcon, s_knw, s_qd, s_cb, s_vp, s_zp = (
            sem(x) for x in ("pads", "bias_con", "new_kv_in", "qd_in", "cb_in", "v_in", "z_in"))
        s_s, s_mx, s_nm, s_p, s_ri, s_pn, s_trp, s_ev, s_pv, s_o, s_ou, s_po = (
            sem(x) for x in ("scores", "row_max", "neg_max", "exp", "rinv", "probs", "p_transposed", "pt",
                             "pv", "o", "out_mm", "out_added"))
        s_dd, s_qn, s_sc, s_dmx, s_gmx, s_gm, s_ex, s_td, s_dv, s_rd, s_ridn, s_od, s_oe, s_oe2, s_to, s_os = (
            sem(x) for x in ("pages_used", "new_scores", "sc_copied", "group_max", "dec_max", "dec_neg_max", "dec_exp",
                             "d_transposed", "ptd", "dec_sum", "dec_rinv", "dec_o", "dec_o_heads", "dec_o_dup",
                             "dec_o_t", "dec_o_done"))
        s_wof, s_oz, s_ys, s_yc, s_yt, s_y = (
            sem(x) for x in ("wof_in", "oz", "ys_mm", "ys", "ys_t", "x3"))
        s_braw, s_m4, s_end = sem("braw_in"), sem("m4_in"), sem("y_out")

        block = ctx.enter_context(nc.Block())

        def paired(eng, n, body):
            for i in (0, 1):
                body(i, i, 0)
            with eng.Fori(1, n // 2 - 1) as i:
                body(2 * i, 0, i)
                body(2 * i + 1, 1, i)
            for i in (n - 2, n - 1):
                body(i, i % 2, i // 2)

        def at(t, i):
            return t[i] if isinstance(i, int) else t[ds(i, 1)].rearrange("x a b -> (x a) b")

        def tile(t, i):
            return t[:, i, :] if isinstance(i, int) else flat(t[:, ds(i, 1), :])

        def decode_rows(t):
            return t[:, SEQ:R].rearrange("p (b t) -> p b t", t=DS)

        def decode_window(ux, j):
            return ux[:, USAMP:UEXT].rearrange("p (b w) -> p b w", w=SW)[:, :, j:j + DS]

        def u_place(ux, r):
            a, b = RCH[r]
            if b <= SEQ:
                return [(ux[:, HIST + a:HIST + b], 0, b - a, False)]
            return [(ux[:, HIST + a:HIST + SEQ], 0, SEQ - a, False),
                    (decode_window(ux, HIST), SEQ - a, R - a, True)]

        def bank(st, r):
            return PS[:, 3 * st + r, :]

        def rows3(ap):
            return ap.rearrange("p (b t) -> p b t", t=DS)

        def evacs(b, t, c=None):
            if t < 0:
                b, t = b - 1, t + 16
            last = 0 if t < 8 else 1
            return 24 * b + (t + 1 if t < 8 else 8 + 2 * (t - 8) + (last if c is None else c) + 1)

        def started(b):
            return not (isinstance(b, int) and b == 0)

        def steps(eng, body):
            body(0, 0, 0)
            body(1, 1, 0)
            with eng.Fori(1, DB // 2) as i:
                body(2 * i, 0, i)
                body(2 * i + 1, 1, i)
            body(DB, 0, DB // 2)

        @block.sync
        def _(sp):
            def raw(u, src, s, n=KD * P):
                atleast(sp, s_lo, u - 1)
                sp.dma_start(RAW[s][:, 0:n], src).then_inc(s_raw[s], 16)

            for k in range(KD):
                sp.dma_start(XIN[:, k, :], xT[:, k, :]).then_inc(s_xin[k], 16)
                if k == 0:
                    sp.dma_start(CST[:], cst).then_inc(s_con, 16)
                    sp.dma_start(FCON[:], fcon).then_inc(s_con, 16)
                    sp.dma_start(PTAB[:], ptab).then_inc(s_pt, 16)
            raw(0, wA[0], 0)
            raw(1, wA[1], 1)
            sp.wait_ge(s_h, KD)
            for arr, dst in ((est, UX[0][:, USAMP:UEXT]), (cw, CWT[0][:])):
                sp.dma_start(dst, arr[0]).then_inc(s_est[0], 16)
            for u in (2, 3, 4):
                raw(u, wA[u], u % 2)

            def past_logf(b, first, n):
                with sp.Fori(first, first + n) as j:
                    page = sp.value_load(PTAB[0:1, ds(NPG * b + j, 1)], min_val=0, max_val=clf.shape[0] - 1)
                    sp.dma_start(lfG[ds(H * b, H), ds(j * PAGE, PAGE)], at(clf, page)).then_inc(s_lfg, 16)

            sp.wait_ge(s_pt, 16)

            def chunk(n, s, i):
                sp.wait_ge(s_u, n + 1)
                sp.dma_start(at(cpT, n), UX[s][:, USAMP - HIST:USAMP]).then_inc(s_cst, 16)
                sp.dma_start(at(csT, n), UX[s][:, USAMP:UEXT]).then_inc(s_cst, 16)
                if not (isinstance(n, int) and n == NCH - 1):
                    atleast(sp, s_cst, 32 * n)
                    atleast(sp, s_c, n)
                    sp.dma_start(UX[1 - s][:, USAMP:UEXT], at(est, n + 1)).then_inc(s_est[1 - s], 16)
                    sp.dma_start(CWT[1 - s][:], at(cw, n + 1)).then_inc(s_est[1 - s], 16)
                for j in (5, 6, 7):
                    u = 3 * n + j
                    if isinstance(u, int) and u == U_OUT + 4:
                        past_logf(i, NPG // 2 * s + 10, 6)
                        break
                    if isinstance(u, int) and u >= U_OUT:
                        raw(u, wO[u - U_OUT], (s + j) % 2)
                    else:
                        raw(u, at(wA, u), (s + j) % 2)
                    past_logf(i, NPG // 2 * s + 5 * (j - 5), 6 if j == 7 else 5)

            paired(sp, NCH, chunk)
            sp.wait_ge(s_zst, 16 * NCH)
            sp.wait_ge(s_mu, 1)
            for n in range(NCH):
                atleast(sp, s_m, n - 1)
                sp.dma_start(Z1[n % 2][:], zT[n]).then_inc(s_z1[n % 2], 16)
            sp.wait_ge(s_ml, NCH)
            sp.dma_start(X2[:], xT).then_inc(s_x1in, 16)
            for u in range(U_OUT + 4, U_PLE):
                raw(u, wO[u - U_OUT], u % 2)
            def ple_loads(l, u0):
                with sp.Fori(0, KD // 2) as i:
                    for s in range(2):
                        raw(u0 + 2 * i + s, at(wP[l], 2 * i + s), (u0 + s) % 2, SLOT)

            ple_loads(0, U_PLE)
            for u in range(U_K, U_K + 2):
                raw(u, wB[u - U_K], u % 2)
            sp.wait_ge(s_lfg, 16 * NPG * DB)
            sp.wait_ge(s_sd2, 1)
            sp.dma_start(LFP[:], lfG).then_inc(s_lfp, 16)
            with sp.Fori(1, 16) as i:
                for s in range(2):
                    raw(U_K + 2 * i + s, at(wB, 2 * i + s), s)
            raw(U_TAIL - 1, wB[U_TAIL - 1 - U_K], 0)

            sp.wait_ge(s_bcon, 1)

            def pages(b):
                for t in range(16):
                    for kk in range(GP):
                        page = sp.value_load(PTAB[0:1, ds(NPG * b + GP * (t % NG) + kk, 1)], min_val=0,
                                             max_val=ck.shape[0] - 1)
                        if kk == 0 and (started(b) or t >= 4):
                            sp.wait_ge(s_dd, 16 * b + t - 3)
                        sp.dma_start(KV[t % 4][:, kk, :], at(ck if t < NG else cv, page)).then_inc(s_kv[t % 4], 16)

            pages(0)
            with sp.Fori(1, DB) as b:
                pages(b)
            sp.wait_ge(s_ys, 1)
            ple_loads(1, U_TAIL)
            for m in range(KD):
                sp.wait_ge(s_x2, KD + m + 1)
                sp.dma_start(yT[:, m, :], X2[:, m, :]).then_inc(s_end, 16)
            sp.wait_ge(s_end, 16 * KD)


        def group(pe, st, s, xh, xl, nk, ready=None, first=True, last=True, off=0, base=0):
            for k in range(nk):
                if ready is not None:
                    pe.wait_ge(ready, base + k + 1 if first else nk + k + 1)
                kk = slice((off + k) * P, (off + k + 1) * P)
                for r, (a, b) in enumerate(RCH):
                    out = bank(st, r)[:, 0:b - a]
                    pe.matmul(out, WH[s][:, kk], xh[:, k, a:b], start=first and k == 0, stop=False)
                    pe.matmul(out, WH[s][:, kk], xl[:, k, a:b], start=False, stop=False)
                    mm = pe.matmul(out, WL[s][:, kk], xh[:, k, a:b], start=False, stop=last and k == nk - 1)
            return mm

        def colsum(pe, st, src, first=True, last=True, w=None):
            for r, (a, b) in enumerate(RCH):
                mm = pe.matmul(bank(st, r)[:, 0:b - a], ONES if w is None else w, src[:, a:b], start=first, stop=last)
            return mm

        @block.tensor
        def _(pe):
            pe.wait_ge(s_con, 32)
            for k in range(KD):
                pe.wait_ge(s_sq0, k + 1)
                colsum(pe, 1, T0[k % 2], k == 0, k == KD - 1).then_inc(s_st0, 1)

            def chunk(n, s, i):
                for kind, (free, v) in enumerate(((s_u, n), (s_zs, n), (s_sg, n + 1))):
                    pe.wait_ge(s_lo, 3 * n + kind + 1)
                    atleast(pe, free, v)
                    if isinstance(n, int) and n == 0 and kind == 1:
                        pe.wait_ge(s_sd0, 1)
                    group(pe, (s + kind) % 2, (s + kind) % 2, HH, HL, KD,
                          ready=s_h if isinstance(n, int) and n == 0 and kind == 0 else None).then_inc(s_unit, 1)

            paired(pe, NCH, chunk)
            pe.wait_ge(s_csum, NCH + 1)
            pe.wait_ge(s_u, NCH)
            colsum(pe, 0, CSUM).then_inc(s_mmu, 1)
            pe.wait_ge(s_zs, NCH)
            for n in range(NCH):
                pe.wait_ge(s_sq1, n + 1)
                colsum(pe, 1, T1[n % 2], n == 0, n == NCH - 1).then_inc(s_var, 1)

            def out0(m, st, ready=None):
                for half in range(2):
                    u = U_OUT + 2 * m + half
                    pe.wait_ge(s_lo, u + 1)
                    if half == 0:
                        if isinstance(m, int) and m < 2:
                            pe.wait_ge((s_mu, s_sd1)[m], 1)
                        else:
                            pe.wait_ge(s_x1, m - 1)
                    group(pe, st, half, MH[:, KD * half:KD * half + KD, :], ML[:, KD * half:KD * half + KD, :], KD,
                          ready=ready, first=half == 0, last=half == 1).then_inc(s_unit, 1)

            out0(0, 0, s_ml)
            out0(1, 1)
            with pe.Fori(1, 4) as i:
                out0(2 * i, 0)
                out0(2 * i + 1, 1)
            def ple(l, u0, free_gate, free_p):
                def unit(m, s, i):
                    first = isinstance(m, int) and m == 0
                    pe.wait_ge(s_lo, u0 + m + 1)
                    pe.wait_ge(*(free_gate if first else (s_sgp, KD * l + m)))
                    group(pe, 0, (u0 + s) % 2, XH, XL, KD, ready=s_xl if first else None,
                          base=KD * l).then_inc(s_gate, 1)
                    pe.wait_ge(*(free_p if first else (s_t2, KD * l + m)))
                    group(pe, 1, (u0 + s) % 2, PH, PL, 2, ready=s_pl if first else None, base=2 * l,
                          off=KD).then_inc(s_unit, 1)
                paired(pe, KD, unit)

            ple(0, U_PLE, (s_x1, KD - 1), (s_x1, KD))

            def main(u, s, st=1, ready=None, base=0):
                pe.wait_ge(s_lo, u + 1)
                group(pe, st, s, GH, GL, KD, ready=ready, base=base).then_inc(s_unit, 1)

            def norm(p):
                pe.wait_ge(s_sq3, p + 1)
                atleast(pe, s_rs, p)
                colsum(pe, 0, SQ3, w=BONES).then_inc(s_n, 1)

            def transposes(m, s):
                if isinstance(m, int) and m == 0:
                    pe.wait_ge(s_rs, PAIRS)
                else:
                    pe.wait_ge(s_vr, m)
                pe.wait_ge(s_kc, PAIRS + m + 1)
                for c in range((R + P - 1) // P):
                    n = min(P, R - c * P)
                    t = pe.transpose(PS[0:n, c // 4, (c % 4) * P:(c % 4 + 1) * P], KC[s][:, c * P:c * P + n], IDENT)
                t.then_inc(s_tr, 1)

            pe.wait_ge(s_ss2, KD + 1)
            pe.wait_ge(s_sgp, KD)
            colsum(pe, 0, SS2).then_inc(s_st2, 1)

            def k_unit(m, s, i):
                first = isinstance(m, int) and m == 0
                pe.wait_ge(*((s_t2, KD) if first else (s_kc, m)))
                main(U_K + m, s, ready=s_gl if first else None)
                if not first:
                    norm(m - 1)

            def v_unit(m, s, i):
                pe.wait_ge(s_kc, PAIRS + m)
                main(U_V + m, s)
                if isinstance(m, int) and m == 0:
                    norm(PAIRS - 1)
                else:
                    transposes(m - 1, 1 - s)

            def q_unit(m, s, i):
                first = isinstance(m, int) and m == 0
                pe.wait_ge(*((s_fl, 1) if first else (s_kc, 2 * PAIRS + m)))
                main(U_Q + m, 1 - s, ready=s_gl if first else None, base=KD)
                if not first:
                    norm(PAIRS + m - 1)

            def z_unit(m, s, i):
                if isinstance(m, int) and m < 2:
                    pe.wait_ge(*((s_kc, 3 * PAIRS), (s_rs, 2 * PAIRS))[m])
                else:
                    pe.wait_ge(s_zc, m - 1)
                main(U_Z + m, 1 - s, st=1 - s)
                if isinstance(m, int) and m == 0:
                    norm(2 * PAIRS - 1)

            paired(pe, PAIRS, k_unit)
            paired(pe, PAIRS, v_unit)
            pe.wait_ge(s_kc, 2 * PAIRS)
            main(U_F, 0)
            transposes(PAIRS - 1, 1)
            paired(pe, PAIRS, q_unit)
            paired(pe, PAIRS, z_unit)

            def att_step(b, par, bh):
                ident = BCON[:, B_ID:B_ID + P]
                for t in range(16):
                    item, hl = t // 2, t % 2
                    prev = started(b) or t > 0
                    real = not (isinstance(b, int) and b == DB)
                    n = P * (item + 1)
                    if real:
                        if t == 0:
                            pe.wait_ge(s_q[par], 80 * (bh + 1))
                        atleast(pe, s_p, 16 * b + t - 1)
                        for c in range((n + 511) // 512):
                            a, e = 512 * c, min(n, 512 * c + 512)
                            out = PS[:, 2 * hl + c, :]
                            pe.matmul(out[:, 0:e - a], BCON[0:96, B_SP + P * hl:B_SP + P * hl + P], CP[par][:, a:e],
                                      start=True, stop=False)
                            if e == n:
                                pe.matmul(out[:, n - P - a:n - a], ident, BCON[:, B_MD:B_MD + P], start=False,
                                          stop=False)
                            mm = pe.matmul(out[:, 0:e - a],
                                           QT[par][HD * hl:HD * hl + HD, P * item:P * item + P],
                                           KT[par][HD * hl:HD * hl + HD, a:e], start=False, stop=True)
                        mm.then_inc(s_s, 1)
                    if prev and (real or t == 0):
                        tp = (t - 1) % 16
                        pe.wait_ge(s_pn, 16 * b + t)
                        nb = tp // 2 + 1
                        for c in range((nb + 3) // 4):
                            if c == 0:
                                atleast(pe, s_ev, evacs(b, t - 2, 0) if started(b) or t > 1 else 0)
                                if started(b):
                                    atleast(pe, s_po, 16 * b - 16 + t)
                            else:
                                atleast(pe, s_ev, evacs(b, t - 2))
                                pe.wait_ge(s_dv, 9 * b if t == 0 else 9 * b + t - 7)
                            for k in range(4 * c, min(nb, 4 * c + 4)):
                                mm = pe.transpose(PS[:, 5 + c, P * (k % 4):P * (k % 4) + P],
                                                  PP[tp % 2][:, P * k:P * k + P], IDENT)
                            mm.then_inc(s_trp, 1)
                    if t == 8 and real:
                        pe.wait_ge(s_ex, 9 * b + 1)
                        atleast(pe, s_os, b)
                        if started(b):
                            pe.wait_ge(s_ev, evacs(b, -1))
                        pe.transpose(PS[:, 6, 0:P], SC[:, PAST:PAST + P], IDENT).then_inc(s_td, 1)
                    if t == 0 and started(b):
                        prompt_pv(b - 1, NQ - 1)
                        pe.wait_ge(s_oe2, b)
                        pe.wait_ge(s_ev, evacs(b, -1))
                        pe.transpose(PS[:, 6, 0:P], OE[:], IDENT).then_inc(s_to, 1)
                    if t < NG and real:
                        if t == 0:
                            atleast(pe, s_od, b)
                            pe.wait_ge(s_qd, 64 * (b + 1))
                            pe.wait_ge(s_cb, 48 * (b + 1) + 48)
                        else:
                            pe.wait_ge(s_sc, 9 * b + t)
                        pe.wait_ge(s_kv[t % 4], 64 * (4 * b + t // 4 + 1))
                        pe.matmul(PS[:, 4, :], BCON[0:96, B_SD:B_SD + P], CB[:, 512 * t:512 * t + 512],
                                  start=True, stop=False)
                        for x in range(2):
                            for j in range(4):
                                p = 2 * j + x
                                mm = pe.matmul(PS[32 * j:32 * j + 32, 4, :], QD[:, p, :],
                                               KV[t % 4][:, :, P * p:P * p + P], start=False, stop=x == 1)
                        mm.then_inc(s_dd, 1)
                    if started(b):
                        half, mo = t // 8, t % 8
                        pe.wait_ge(s_ev, evacs(b, t - 1, 0) if real or t == 0 else evacs(b, -1))
                        if t == 0:
                            pe.wait_ge(s_wo[1 - par], 16 * (bh + (1 if par else 0)))
                            pe.wait_ge(s_o, NQ * b - 4)
                        if t == 8:
                            pe.wait_ge(s_o, NQ * b)
                        if not real or t == 0:
                            atleast(pe, s_po, 16 * b - 16 + t)
                        pe.matmul(PS[:, 5, :], WOP[1 - par][:, P * mo:P * mo + P],
                                  OP[1 - par][:, 512 * half:512 * half + 512], start=True, stop=True).then_inc(s_ou, 1)
                    if not real:
                        continue
                    if t >= 2 and hl == 0:
                        prompt_pv(b, item - 1)
                    if t == NG - 1:
                        pe.wait_ge(s_sc, 9 * b + NG)
                        out = PS[:, 4, 0:RS]
                        pe.matmul(out, BCON[0:96, B_SD:B_SD + P], CB[:, PAST:PAST + RS], start=True, stop=False)
                        mn = BCON[:, B_MN + RS * b:B_MN + RS * b + RS] if isinstance(b, int) else \
                            BCON[:, ds(B_MN + RS * b, RS)]
                        pe.matmul(out, ident, mn, start=False, stop=False)
                        for x in range(2):
                            for j in range(4):
                                p = 2 * j + x
                                mm = pe.matmul(PS[32 * j:32 * j + 32, 4, 0:RS], QD[:, p, :], KNW[:, p, :],
                                               start=False, stop=x == 1)
                        mm.then_inc(s_qn, 1)
                    if t >= NG:
                        j = t - NG
                        pe.wait_ge(s_ex, 9 * b + j + 2)
                        pe.wait_ge(s_dv, 9 * b + j + 1)
                        pe.wait_ge(s_ev, evacs(b, t - 1))
                        for kk in range(GP):
                            mm = pe.transpose(PS[:, 6, P * kk:P * kk + P],
                                              SC[:, 512 * j + P * kk:512 * j + P * kk + P], IDENT)
                        mm.then_inc(s_td, 1)
                        if j == 0:
                            pe.wait_ge(s_sc, 9 * b + NG + 1)
                        pe.wait_ge(s_dv, 9 * b + j + 2)
                        pe.wait_ge(s_kv[t % 4], 64 * (4 * b + t // 4 + 1))
                        for kk in range(GP):
                            for g in range(4):
                                mm = pe.matmul(PS[32 * g:32 * g + 32, 4, 0:4 * HD], PTD[j % 2][:, kk, 32 * g:32 * g + 32],
                                               KV[t % 4][:, kk, 4 * HD * g:4 * HD * g + 4 * HD], start=j == 0 and kk == 0,
                                               stop=j == NG - 1 and kk == GP - 1)
                            if j == kk == 0:
                                for g in range(4):
                                    pe.matmul(PS[32 * g:32 * g + 32, 4, 0:4 * HD], PTN[:, 32 * g:32 * g + 32],
                                              VNW[:, 4 * HD * g:4 * HD * g + 4 * HD], start=False, stop=False)
                        mm.then_inc(s_dd, 1)

            def prompt_pv(b, i):
                pe.wait_ge(s_ev, evacs(b, 2 * i + 1))
                atleast(pe, s_o, NQ * b + i)
                if i == 0:
                    pe.wait_ge(s_vp, 16 * (b + 1))
                for k in range(i + 1):
                    for hl in range(2):
                        mm = pe.matmul(PS[HD * hl:HD * hl + HD, 7, 0:P], VP[:, k, HD * hl:HD * hl + HD],
                                       PT[hl][:, P * k:P * k + P], start=k == 0, stop=k == i)
                mm.then_inc(s_pv, 1)

            pe.wait_ge(s_bcon, 1)
            pe.wait_ge(s_pad2, 5)
            pe.wait_ge(s_knw, 32)
            pe.wait_ge(s_zc, PAIRS)
            steps(pe, att_step)

            pe.wait_ge(s_wof, 16)
            pe.wait_ge(s_oz, 1)
            for c in range(2):
                for p in range(PAIRS):
                    mm = pe.matmul(PS[0:RS, c, :], OS[:, p, :], WOF[:, p, 512 * c:512 * c + 512], start=p == 0,
                                   stop=p == PAIRS - 1)
            mm.then_inc(s_ys, 1)
            pe.wait_ge(s_yc, 1)
            for k in range(KD):
                mm = pe.transpose(PS[:, 2, RS * k:RS * k + RS], YS[:, P * k:P * k + P], FCON[0:RS, 0, 0:RS])
            mm.then_inc(s_yt, 1)
            pe.wait_ge(s_y, 1)
            ple(1, U_TAIL, (s_y, 1), (s_y, 1))


        @block.scalar
        def _(act):
            def hi(u, half_u, s, n=KD * P):
                act.wait_ge(s_raw[s], 16 * half_u + 16)
                atleast(act, s_unit, u - 1)
                act.activation(WH[s][:, 0:n], RAW[s][:, 0:n], ACT.Copy).then_inc(s_hi, 1)

            act.wait_ge(s_con, 32)
            for k in range(KD):
                act.wait_ge(s_xin[k], 16)
                atleast(act, s_st0, k - 1)
                act.activation(T0[k % 2][:], XIN[:, k, :], ACT.Square).then_inc(s_sq0, 1)
            hi(0, 0, 0)
            hi(1, 0, 1)
            act.wait_ge(s_st0, KD)
            for r, (a, b) in enumerate(RCH):
                i = act.activation(RSTD0[:, a:b], bank(1, r)[:, 0:b - a], ACT.Sqrt, scale=1.0 / D,
                                   bias=CST[:, C_EPS:C_EPS + 1])
            i.then_inc(s_sd0, 1)
            for k in range(KD):
                act.wait_ge(s_t0, k + 1)
                act.activation(HH[:, k, :], T0[k % 2][:], ACT.Copy).then_inc(s_hh, 1)

            def sigmoid_b(n, s, fills):
                act.wait_ge(s_est[s], 32 * fills)
                act.wait_ge(s_unit, 3 * n + 1)
                for r, (a, b) in enumerate(RCH):
                    for dst, x, y, dec in u_place(UX[s], r):
                        src = bank(s, r)[:, x:y]
                        i = act.activation(dst, rows3(src) if dec else src, ACT.Sigmoid)
                i.then_inc(s_sg, 1)

            act.wait_ge(s_pad, 2)
            sigmoid_b(0, 0, 1)
            hi(2, 1, 0)

            def products(n, s, qs):
                for q in qs:
                    if q == 0:
                        act.wait_ge(s_u, n + 1)
                    atleast(act, s_add, n * (NT - 1) + {0: -1, 1: 0, 2: 1}.get(q, q - 2))
                    j = NV + q
                    o = PROD[(s * NT + q) % 2]
                    act.activation(o[:, 0:SEQ], UX[s][:, j:j + SEQ], ACT.Copy, scale=CWT[s][:, j:j + 1])
                    act.activation(decode_rows(o), decode_window(UX[s], j), ACT.Copy,
                                   scale=CWT[s][:, j:j + 1]).then_inc(s_prod, 1)

            def chunk(n, s, i):
                last = isinstance(n, int) and n == NCH - 1
                hu = [3 * i + (3 * s + j) // 2 for j in (3, 4, 5)]
                hi(3 * n + 3, hu[0], (s + 3) % 2)
                products(n, s, range(0, 4))
                atleast(act, s_zst, 16 * n)
                act.wait_ge(s_unit, 3 * n + 3)
                for r, (a, b) in enumerate(RCH):
                    z = act.activation(ZS[:, a:b], bank(s, r)[:, 0:b - a], ACT.Silu)
                z.then_inc(s_zs, 1)
                act.wait_ge(s_zs, n + 1)
                act.dma_start(at(zT, n), ZS[:]).then_inc(s_zst, 16)
                hi(3 * n + 4, hu[1], (s + 4) % 2)
                products(n, s, range(4, 7))
                if not last:
                    sigmoid_b(n + 1, 1 - s, i + 1 + s)
                    hi(3 * n + 5, hu[2], (s + 5) % 2)
                products(n, s, range(7, NT))

            paired(act, NCH, chunk)
            act.wait_ge(s_mmu, 1)
            act.wait_ge(s_cst, 32 * NCH)
            act.wait_ge(s_zst, 16 * NCH)
            for r, (a, b) in enumerate(RCH):
                i = act.activation(MU[:, a:b], bank(0, r)[:, 0:b - a], ACT.Copy, scale=1.0 / EA)
            i.then_inc(s_mu, 1)
            for n in range(NCH):
                act.wait_ge(s_xc, n + 1)
                atleast(act, s_var, n - 1)
                act.activation(T1[n % 2][:], CC[:, n, :], ACT.Square).then_inc(s_sq1, 1)
            act.wait_ge(s_var, NCH)
            for r, (a, b) in enumerate(RCH):
                i = act.activation(MU[:, a:b], bank(1, r)[:, 0:b - a], ACT.Sqrt, scale=1.0 / EA,
                                   bias=CST[:, C_EPS:C_EPS + 1])
            i.then_inc(s_sd1, 1)
            for n in range(NCH + 1):
                if n < NCH:
                    act.wait_ge(s_t1, n + 1)
                    atleast(act, s_m, n - 1)
                    act.activation(Y1[n % 2][:], T1[n % 2][:], ACT.Silu, bias=CST[:, C_LB + n:C_LB + n + 1],
                                   scale=CST[:, C_LG + n:C_LG + n + 1]).then_inc(s_y1, 1)
                if n > 0:
                    act.wait_ge(s_m, n)
                    act.activation(MH[:, n - 1, :], T1[(n - 1) % 2][:], ACT.Copy).then_inc(s_mh, 1)
            with act.Fori(0, 7) as i:
                hi(2 * i + 50, i + 25, 0)
                hi(2 * i + 51, i + 25, 1)
            def hi_next(u0, s, i, n=KD * P):
                hi(u0 + 2 * i + s + 1, i + (u0 + s + 1) // 2, (u0 + s + 1) % 2, n)

            def square2(m):
                act.wait_ge(s_x2, m + 1)
                act.wait_ge(s_ss2, m + 1)
                act.activation(SQ2[:], tile(X2, m), ACT.Square).then_inc(s_sq2, 1)

            def ple(l, u0):
                act.dma_start(PR[:], pT[l]).then_inc(s_prin, 16)
                for k in range(KD):
                    if l == 0:
                        act.wait_ge(s_x1, k + 1)
                    act.activation(XH[:, k, :], X2[:, k, :], ACT.Copy).then_inc(s_xh, 1)
                    if k == 1:
                        act.wait_ge(s_prin, 16 * (l + 1))
                        for j in range(2):
                            act.activation(PH[:, j, :], PR[:, j, :], ACT.Copy).then_inc(s_ph, 1)

                def unit(m, s, i):
                    end = isinstance(m, int) and m == KD - 1
                    if not (end and l == 1):
                        hi_next(u0, s, i, KD * P if end else SLOT)
                    act.wait_ge(s_gate, KD * l + m + 1)
                    atleast(act, s_t2, KD * l + m)
                    for r, (a, b) in enumerate(RCH):
                        g = act.activation(SG[:, a:b], bank(0, r)[:, 0:b - a], ACT.Sigmoid)
                    g.then_inc(s_sgp, 1)
                    if l == 0 and not (isinstance(m, int) and m == 0):
                        square2(m - 1)
                paired(act, KD, unit)

            hi(U_PLE, U_PLE // 2, 0, SLOT)
            act.wait_ge(s_unit, U_PLE)
            ple(0, U_PLE)
            square2(KD - 1)
            act.wait_ge(s_st2, 1)
            for r, (a, b) in enumerate(RCH):
                g = act.activation(RSTD2[:, a:b], bank(0, r)[:, 0:b - a], ACT.Sqrt, scale=1.0 / D,
                                   bias=CST[:, C_EPS:C_EPS + 1])
            g.then_inc(s_sd2, 1)

            def h_hi(base):
                for k in range(KD):
                    act.wait_ge(s_g, base + k + 1)
                    act.activation(GH[:, k, :], (KN, SQ3)[k % 2][:], ACT.Copy).then_inc(s_gh, 1)

            def copy_out(u, s):
                act.wait_ge(s_unit, u + 1)
                for r, (a, b) in enumerate(RCH):
                    g = act.activation(KC[s][:, a:b], bank(1, r)[:, 0:b - a], ACT.Copy)
                g.then_inc(s_kc, 1)

            def norm(p, keys=True):
                act.wait_ge(s_n, p + 1)
                atleast(act, s_kn, p)
                scale, eps = (1.0 / HD, C_EPS) if keys else (1.0, C_EPQ)
                for r, (a, b) in enumerate(RCH):
                    g = act.activation(RS3[:, a:b], bank(0, r)[:, 0:b - a], ACT.Sqrt, scale=scale,
                                       bias=CST[:, eps:eps + 1])
                g.then_inc(s_rs, 1)

            def square3(p, s, copies):
                atleast(act, s_n, p)
                act.wait_ge(s_kc, copies)
                act.activation(SQ3[:], KC[s][:], ACT.Square).then_inc(s_sq3, 1)

            def k_unit(m, s, i):
                hi_next(U_K, s, i)
                atleast(act, s_kn, m - 1)
                copy_out(U_K + m, s)
                if not (isinstance(m, int) and m == 0):
                    norm(m - 1)
                square3(m, s, m + 1)

            def v_unit(m, s, i):
                hi_next(U_V, s, i)
                if isinstance(m, int) and m < 2:
                    act.wait_ge(s_kn, PAIRS - 1 + m)
                else:
                    act.wait_ge(s_tr, m - 1)
                copy_out(U_V + m, s)
                if isinstance(m, int) and m == 0:
                    norm(PAIRS - 1)

            def q_unit(m, s, i):
                hi_next(U_Q, s, i)
                if isinstance(m, int) and m < 2:
                    act.wait_ge(s_tr, PAIRS - 1 + m)
                else:
                    act.wait_ge(s_kn, PAIRS + m - 1)
                copy_out(U_Q + m, s)
                if not (isinstance(m, int) and m == 0):
                    norm(PAIRS + m - 1, keys=False)
                square3(PAIRS + m, s, 2 * PAIRS + m + 1)

            def z_unit(m, s, i):
                if not (isinstance(m, int) and m == PAIRS - 1):
                    hi_next(U_Z, s, i)
                if isinstance(m, int) and m < 2:
                    act.wait_ge(s_kn, 2 * PAIRS - 1 + m)
                else:
                    act.wait_ge(s_gst[s], 16 * i)
                act.wait_ge(s_unit, U_Z + m + 1)
                for r, (a, b) in enumerate(RCH):
                    g = act.activation(KC[s][:, a:b], bank(1 - s, r)[:, 0:b - a], ACT.Silu)
                g.then_inc(s_zc, 1)
                if isinstance(m, int) and m == 0:
                    norm(2 * PAIRS - 1, keys=False)
                if isinstance(m, int) and m == 1:
                    act.wait_ge(s_f, 1)
                    act.activation(SQ3[0:H, :], SQ3[0:H, :], ACT.Exp).then_inc(s_fe, 1)

            h_hi(0)
            paired(act, PAIRS, k_unit)
            paired(act, PAIRS, v_unit)
            hi(U_Q, U_Q // 2, U_Q % 2)
            act.wait_ge(s_unit, U_F + 1)
            for r, (a, b) in enumerate(RCH):
                g = act.activation(FL[0:H, a:b], bank(1, r)[0:H, 0:b - a], ACT.Identity,
                                   bias=CST[0:H, C_FB:C_FB + 1])
            g.then_inc(s_fl, 1)
            h_hi(KD)
            paired(act, PAIRS, q_unit)
            paired(act, PAIRS, z_unit)

            def att_step(b, par, bh):
                real = not (isinstance(b, int) and b == DB)
                for t in range(16 if real else 1):
                    item, hl = t // 2, t % 2
                    if t == NG:
                        act.wait_ge(s_qn, b + 1)
                        act.activation(SC[:, PAST:PAST + RS], PS[:, 4, 0:RS], ACT.Copy).then_inc(s_sc, 1)
                    if started(b) or t > 0:
                        tp = (t - 1) % 16
                        bb = b if t else b - 1
                        n = P * (tp // 2 + 1)
                        atleast(act, s_pv, NQ * bb + tp // 2)
                        for c in range((n + 511) // 512):
                            a, e = 512 * c, min(n, 512 * c + 512)
                            act.wait_ge(s_trp, evacs(bb, tp, c))
                            act.activation(PT[tp % 2][:, a:e], PS[:, 5 + c, 0:e - a], ACT.Copy).then_inc(s_ev, 1)
                    if not real:
                        continue
                    n = P * (item + 1)
                    act.wait_ge(s_nm, 16 * b + t + 1)
                    atleast(act, s_trp, evacs(b, t - 2) if started(b) or t > 1 else 0)
                    act.activation(PP[hl][:, 0:n], PS[:, 2 * hl:2 * hl + 2, :].rearrange("p a n -> p (a n)")[:, 0:n],
                                   ACT.Exp, bias=NMX[hl][:], accum_out=SMP[hl][:]).then_inc(s_p, 1)
                    if t < NG:
                        act.wait_ge(s_dd, 16 * b + t + 1)
                        atleast(act, s_td, 9 * b)
                        act.activation(SC[:, 512 * t:512 * t + 512], PS[:, 4, :], ACT.Copy).then_inc(s_sc, 1)
                        continue
                    j = t - NG
                    if j == 0:
                        act.wait_ge(s_gm, b + 1)
                        atleast(act, s_rd, b)
                        dec_exp(NG)
                        dec_exp(0)
                        act.wait_ge(s_td, 9 * b + 1)
                        atleast(act, s_dd, 16 * b)
                        act.activation(PTN[:], PS[0:RS, 6, 0:P], ACT.Copy).then_inc(s_dv, 1)
                    if j < NG - 1:
                        dec_exp(j + 1)
                    act.wait_ge(s_td, 9 * b + j + 2)
                    act.wait_ge(s_dd, 16 * b + t - 1)
                    act.activation(PTD[j % 2][:], PS[:, 6, :].rearrange("p (k n) -> p k n", n=P),
                                   ACT.Copy).then_inc(s_dv, 1)

            def dec_exp(c):
                a, e = (512 * c, 512 * c + 512) if c < NG else (PAST, PAST + RS)
                act.activation(SC[:, a:e], SC[:, a:e], ACT.Exp, bias=NGM[:],
                               accum_out=SMD[:, c:c + 1]).then_inc(s_ex, 1)

            steps(act, att_step)

            act.wait_ge(s_ys, 1)
            act.activation(YS[:], PS[0:RS, 0:2, :].rearrange("p a n -> p (a n)"), ACT.Copy).then_inc(s_yc, 1)
            hi(U_TAIL, U_TAIL // 2, U_TAIL % 2, SLOT)
            act.wait_ge(s_y, 1)
            ple(1, U_TAIL)


        @block.gpsimd
        def _(pool):
            def lo(u, s, n=KD * P):
                pool.wait_ge(s_hi, u + 1)
                pool.tensor_tensor(WL[s][:, 0:n], RAW[s][:, 0:n], WH[s][:, 0:n].bitcast(F32),
                                   ALU.subtract).then_inc(s_lo, 1)

            lo(0, 0)
            lo(1, 1)
            pool.wait_ge(s_h, KD)
            for s in range(2):
                pool.memset(UX[s][:, 0:HIST], 0.0).then_inc(s_pad, 1)
            pool.memset(CSUM[:], 0.0).then_inc(s_csum, 1)
            lo(2, 0)

            def adds(n, s, qs):
                for q in qs:
                    pool.wait_ge(s_prod, n * NT + q + 1)
                    if q == 1:
                        atleast(pool, s_c, n)
                        pool.tensor_tensor(ACC[:], PROD[(s * NT) % 2][:], PROD[(s * NT + 1) % 2][:],
                                           ALU.add).then_inc(s_add, 1)
                    else:
                        pool.wait_ge(s_add, n * (NT - 1) + q - 1)
                        pool.tensor_tensor(ACC[:], ACC[:], PROD[(s * NT + q) % 2][:], ALU.add).then_inc(s_add, 1)

            def csum(n):
                pool.wait_ge(s_c, n + 1)
                pool.wait_ge(s_csum, n + 1)
                src = tile(CC, n)
                pool.tensor_tensor(CSUM[:], CSUM[:], src, ALU.add).then_inc(s_csum, 1)

            def chunk(n, s, i):
                last = isinstance(n, int) and n == NCH - 1
                lo(3 * n + 3, (s + 3) % 2)
                if not (isinstance(n, int) and n == 0):
                    csum(n - 1)
                adds(n, s, range(1, 4))
                lo(3 * n + 4, (s + 4) % 2)
                adds(n, s, range(4, 7))
                if not last:
                    lo(3 * n + 5, (s + 5) % 2)
                adds(n, s, range(7, NT))

            paired(pool, NCH, chunk)
            csum(NCH - 1)
            for n in range(NCH):
                pool.wait_ge(s_mh, n + 1)
                pool.tensor_tensor(ML[:, n, :], T1[n % 2][:], MH[:, n, :].bitcast(F32),
                                   ALU.subtract).then_inc(s_ml, 1)
            with pool.Fori(0, 7) as i:
                lo(2 * i + 50, 0)
                lo(2 * i + 51, 1)
            def lo_next(u0, s, i, n=KD * P):
                lo(u0 + 2 * i + s + 1, (u0 + s + 1) % 2, n)

            def add2(m):
                pool.wait_ge(s_sq2, m + 1)
                pool.wait_ge(s_ss2, m + 1)
                pool.tensor_tensor(SS2[:], SS2[:], SQ2[:], ALU.add).then_inc(s_ss2, 1)

            def ple(l, u0):
                for j in range(2):
                    pool.wait_ge(s_ph, 2 * l + j + 1)
                    pool.tensor_tensor(PL[:, j, :], PR[:, j, :], PH[:, j, :].bitcast(F32),
                                       ALU.subtract).then_inc(s_pl, 1)
                if l == 0:
                    pool.memset(SS2[:], 0.0).then_inc(s_ss2, 1)

                def unit(m, s, i):
                    end = isinstance(m, int) and m == KD - 1
                    if not (end and l == 1):
                        lo_next(u0, s, i, KD * P if end else SLOT)
                    if l == 0 and not (isinstance(m, int) and m == 0):
                        add2(m - 1)
                paired(pool, KD, unit)

            lo(U_PLE, 0, SLOT)
            ple(0, U_PLE)
            add2(KD - 1)

            def store_kn(p, dst):
                pool.wait_ge(s_kn, p + 1)
                pool.dma_start(dst, KN[:]).then_inc(s_kst, 16)

            def store_v(m):
                cols = slice(m * P, m * P + P) if isinstance(m, int) else ds(m * P, P)
                pool.wait_ge(s_vr, m + 1)
                pool.dma_start(vR[0:SEQ, cols].rearrange("(c p) n -> p c n", p=P), VR[:, 0:SEQ // P, :]).then_inc(s_vst, 16)
                pool.dma_start(vR[SEQ:R, cols], VR[0:RS, SEQ // P, :]).then_inc(s_vst, 16)

            def store_g(m, s):
                pool.wait_ge(s_zc, m + 1)
                pool.dma_start(at(gT, m), KC[s][:]).then_inc(s_gst[s], 16)

            def store_past(c, s):
                cols = slice(c * 512, c * 512 + 512) if isinstance(c, int) else ds(c * 512, 512)
                pool.wait_ge(s_pb, c + 1)
                pool.dma_start(cPa[:, :, cols].rearrange("x h n -> h x n"), PB[s][:]).then_inc(s_pst[s], 16)

            def k_unit(m, s, i):
                lo_next(U_K, s, i)
                if not (isinstance(m, int) and m == 0):
                    store_kn(m - 1, at(kT, m - 1))

            def v_unit(m, s, i):
                lo_next(U_V, s, i)
                if isinstance(m, int) and m == 0:
                    store_kn(PAIRS - 1, kT[PAIRS - 1])
                else:
                    store_v(m - 1)

            def q_unit(m, s, i):
                lo_next(U_Q, s, i)
                if not (isinstance(m, int) and m == 0):
                    store_kn(PAIRS + m - 1, at(qT, m - 1))

            def z_unit(m, s, i):
                if not (isinstance(m, int) and m == PAIRS - 1):
                    lo_next(U_Z, s, i)
                if isinstance(m, int) and m == 0:
                    store_kn(2 * PAIRS - 1, qT[PAIRS - 1])
                else:
                    store_g(m - 1, 1 - s)
                if not (isinstance(m, int) and m < 2):
                    store_past(m - 2, s)

            paired(pool, PAIRS, k_unit)
            paired(pool, PAIRS, v_unit)
            lo(U_Q, U_Q % 2)
            store_v(PAIRS - 1)
            paired(pool, PAIRS, q_unit)
            paired(pool, PAIRS, z_unit)
            store_g(PAIRS - 1, 1)
            store_past(6, 0)
            store_past(7, 1)
            pool.wait_ge(s_f, F_STEPS)
            pool.dma_start(lfT, FL[0:H, :]).then_inc(s_fst, 16)
            pool.dma_start(cPr.rearrange("x h n -> h x n"), FPB[:, :, 0:SEQ]).then_inc(s_fst, 16)
            pool.dma_start(cNw.rearrange("x h n -> h x n"), FPB[:, :, SEQ:R]).then_inc(s_fst, 16)

            pool.wait_ge(s_unit, U_TAIL)
            for s in range(2):
                pool.wait_ge(s_gst[s], 16 * PAIRS // 2)
                pool.wait_ge(s_pst[s], 64)
            pool.wait_ge(s_fst, 48)
            pool.wait_ge(s_kst, 32 * PAIRS)
            pool.wait_ge(s_vst, 32 * PAIRS)
            for s in range(2):
                pool.memset(CP[s][:], 0.0).then_inc(s_pad2, 1)
            pool.memset(QD[:], 0.0).then_inc(s_pad2, 1)
            pool.memset(CB[:], 0.0).then_inc(s_pad2, 1)
            pool.memset(SC[:, PAST + RS:], 0.0).then_inc(s_pad2, 1)
            pool.dma_start(BRAW[:], bcon[:, 0:B_BF]).then_inc(s_braw, 16)
            pool.dma_start(M4[:], bcon[:, B_M4:B_N]).then_inc(s_m4, 16)
            pool.wait_ge(s_braw, 16)
            pool.tensor_copy(BCON[:], BRAW[:]).then_inc(s_bcon, 1)
            pool.wait_ge(s_pad2, 5)

            def load_kq(b, par):
                pool.dma_start(KT[par][:], row(kT, b, 0, SEQ)).then_inc(s_q[par], 16)
                pool.dma_start(QT[par][:], row(qT, b, 0, SEQ)).then_inc(s_q[par], 16)
                hs = slice(2 * b, 2 * b + 2) if isinstance(b, int) else ds(2 * b, 2)
                for x in range(3):
                    pool.dma_start(CP[par][32 * x:32 * x + 2, :], cPr[x, hs, :]).then_inc(s_q[par], 16)

            def load_qc(b):
                cols = slice(SEQ + DS * b, SEQ + DS * b + DS) if isinstance(b, int) else ds(SEQ + DS * b, DS)
                for x in range(2):
                    for hl in range(2):
                        dst = QD[HD * hl:HD * hl + HD, :, :].rearrange("p (j x) n -> p j x n", x=2)[
                            :, :, x, 16 * x + DS * hl:16 * x + DS * hl + DS]
                        src = qT.rearrange("(j x) p n -> p j x n", x=2)[HD * hl:HD * hl + HD, :, x, cols]
                        pool.dma_start(dst, src).then_inc(s_qd, 16)
                hs = slice(H * b, H * b + H) if isinstance(b, int) else ds(H * b, H)
                for x in range(3):
                    pool.dma_start(CB[32 * x:32 * x + H, 0:PAST], cPa[x, hs, :]).then_inc(s_cb, 16)

            def row(t, i, a, e):
                return t[i, :, a:e] if isinstance(i, int) else t[ds(i, 1), :, a:e].rearrange("x a b -> (x a) b")

            load_kq(0, 0)
            for x in range(3):
                pool.dma_start(CB[32 * x:32 * x + H, PAST:PAST + RS], cNw[x]).then_inc(s_cb, 16)
            load_qc(0)
            pool.dma_start(KNW[:], kT[:, :, SEQ:R].rearrange("a p n -> p a n")).then_inc(s_knw, 16)
            pool.dma_start(VNW[:], vR[SEQ:R, :]).then_inc(s_knw, 16)

            def att_step(b, par, bh):
                cols = slice(P * b, P * b + P) if isinstance(b, int) else ds(P * b, P)
                atleast(pool, s_o, NQ * b)
                pool.dma_start(VP[:], vR[0:SEQ, cols].rearrange("(c p) n -> p c n", p=P)).then_inc(s_vp, 16)
                pool.dma_start(ZP[:], row(gT, b, 0, SEQ)).then_inc(s_zp, 16)
                last = isinstance(b, int) and b == DB - 1
                if not last:
                    atleast(pool, s_s, 16 * b)
                    load_kq(b + 1, 1 - par)
                if started(b) and not (isinstance(b, int) and b == 1):
                    pool.wait_ge(s_ou, 16 * b - 16)
                pool.dma_start(WOP[par][:], at(wW, b)).then_inc(s_wo[par], 16)
                if not last:
                    pool.wait_ge(s_qn, b + 1)
                    load_qc(b + 1)

            paired(pool, DB, att_step)

            pool.wait_ge(s_dd, 16 * DB)
            pool.dma_start(WOF[:], wW.rearrange("a p n -> p a n")).then_inc(s_wof, 16)
            pool.dma_start(ZSM[:], gT[:, :, SEQ:R].rearrange("a p n -> p a n")).then_inc(s_wof, 16)
            lo(U_TAIL, U_TAIL % 2, SLOT)
            ple(1, U_TAIL)


        @block.vector
        def _(dve):
            dve.wait_ge(s_sd0, 1)
            dve.reciprocal(RSTD0[:], RSTD0[:]).then_inc(s_rc0, 1)
            dve.wait_ge(s_rc0, 1)
            for k in range(KD + 1):
                if k < KD:
                    atleast(dve, s_h, k - 1)
                    dve.scalar_tensor_tensor(out=T0[k % 2][:], in0=XIN[:, k, :], scalar=CST[:, C_AN + k:C_AN + k + 1],
                                             in1=RSTD0[:], op0=ALU.mult, op1=ALU.mult).then_inc(s_t0, 1)
                if k > 0:
                    dve.wait_ge(s_hh, k)
                    dve.tensor_tensor(HL[:, k - 1, :], T0[(k - 1) % 2][:], HH[:, k - 1, :].bitcast(F32),
                                      ALU.subtract).then_inc(s_h, 1)

            def chunk(n, s, i):
                dve.wait_ge(s_sg, n + 1)
                dve.wait_ge(s_unit, 3 * n + 2)
                for r, (a, b) in enumerate(RCH):
                    for dst, x, y, dec in u_place(UX[s], r):
                        src = bank(1 - s, r)[:, x:y]
                        i = dve.tensor_tensor(dst, rows3(src) if dec else src, dst, ALU.mult)
                i.then_inc(s_u, 1)
                dve.wait_ge(s_u, n + 1)
                w = CWT[s]
                for j in range(NV):
                    for part, (o, x) in enumerate(((CHAIN[:, 0:SEQ], UX[s][:, j:j + SEQ]),
                                                   (decode_rows(CHAIN), decode_window(UX[s], j)))):
                        if j == 0:
                            i = dve.tensor_scalar(o, x, w[:, 0:1], w[:, CW:CW + 1], ALU.mult, ALU.add)
                        else:
                            dve.wait_ge(s_tap, 2 * NV * n + 2 * (j - 1) + part + 1)
                            i = dve.scalar_tensor_tensor(out=o, in0=x, scalar=w[:, j:j + 1], in1=o,
                                                         op0=ALU.mult, op1=ALU.add)
                        i.then_inc(s_tap, 1)
                dve.wait_ge(s_tap, 2 * NV * (n + 1))
                dve.wait_ge(s_add, (n + 1) * (NT - 1))
                o = tile(CC, n)
                dve.tensor_tensor(o, CHAIN[:], ACC[:], ALU.add).then_inc(s_c, 1)

            paired(dve, NCH, chunk)
            dve.wait_ge(s_mu, 1)
            for n in range(NCH):
                dve.wait_ge(s_c, n + 1)
                dve.tensor_tensor(CC[:, n, :], CC[:, n, :], MU[:], ALU.subtract).then_inc(s_xc, 1)
            dve.wait_ge(s_sd1, 1)
            dve.reciprocal(MU[:], MU[:]).then_inc(s_rc1, 1)
            dve.wait_ge(s_rc1, 1)
            for n in range(NCH + 1):
                if n < NCH:
                    atleast(dve, s_ml, n - 1)
                    dve.wait_ge(s_xc, n + 1)
                    dve.tensor_tensor(T1[n % 2][:], CC[:, n, :], MU[:], ALU.mult).then_inc(s_t1, 1)
                if n > 0:
                    dve.wait_ge(s_y1, n)
                    dve.wait_ge(s_z1[(n - 1) % 2], 16 * ((n - 1) // 2 + 1))
                    dve.tensor_tensor(T1[(n - 1) % 2][:], Y1[(n - 1) % 2][:], Z1[(n - 1) % 2][:],
                                      ALU.mult).then_inc(s_m, 1)
            dve.wait_ge(s_x1in, 16)

            def out0(m, st):
                dve.wait_ge(s_unit, U_OUT + 2 * m + 2)
                x = tile(X2, m)
                for r, (a, b) in enumerate(RCH):
                    i = dve.tensor_tensor(x[:, a:b], bank(st, r)[:, 0:b - a], x[:, a:b], ALU.add)
                i.then_inc(s_x1, 1)

            with dve.Fori(0, 4) as i:
                out0(2 * i, 0)
                out0(2 * i + 1, 1)
            def ple(l, u0):
                for k in range(KD):
                    dve.wait_ge(s_xh, KD * l + k + 1)
                    dve.tensor_tensor(XL[:, k, :], X2[:, k, :], XH[:, k, :].bitcast(F32),
                                      ALU.subtract).then_inc(s_xl, 1)

                def unit(m, s, i):
                    dve.wait_ge(s_sgp, KD * l + m + 1)
                    atleast(dve, s_x2, KD * l + m)
                    dve.wait_ge(s_unit, u0 + m + 1)
                    for r, (a, b) in enumerate(RCH):
                        t = dve.tensor_tensor(T2[:, a:b], bank(1, r)[:, 0:b - a], SG[:, a:b], ALU.mult)
                    t.then_inc(s_t2, 1)
                    dve.wait_ge(s_t2, KD * l + m + 1)
                    x = tile(X2, m)
                    dve.tensor_tensor(x, x, T2[:], ALU.add).then_inc(s_x2, 1)
                paired(dve, KD, unit)

            ple(0, U_PLE)
            dve.wait_ge(s_sd2, 1)
            dve.reciprocal(RSTD2[:], RSTD2[:]).then_inc(s_rc2, 1)
            dve.wait_ge(s_rc2, 1)

            def h_split(base, gain):
                for k in range(KD + 1):
                    if k < KD:
                        atleast(dve, s_gl, base + k - 1 if k > 1 or base else 0)
                        dve.scalar_tensor_tensor(out=(KN, SQ3)[k % 2][:], in0=X2[:, k, :],
                                                 scalar=CST[:, gain + k:gain + k + 1],
                                                 in1=RSTD2[:], op0=ALU.mult, op1=ALU.mult).then_inc(s_g, 1)
                    if k > 0:
                        dve.wait_ge(s_gh, base + k)
                        dve.tensor_tensor(GL[:, k - 1, :], (KN, SQ3)[(k - 1) % 2][:], GH[:, k - 1, :].bitcast(F32),
                                          ALU.subtract).then_inc(s_gl, 1)

            def norm(p, s, gain):
                dve.wait_ge(s_rs, p + 1)
                dve.reciprocal(RS3[:], RS3[:]).then_inc(s_rc, 1)
                dve.wait_ge(s_rc, p + 1)
                atleast(dve, s_kst, 16 * p)
                dve.scalar_tensor_tensor(out=KN[:], in0=KC[s][:], scalar=CST[:, gain:gain + 1], in1=RS3[:],
                                         op0=ALU.mult, op1=ALU.mult).then_inc(s_kn, 1)

            def rows_first(m):
                dve.wait_ge(s_tr, m + 1)
                if isinstance(m, int) and m == 0:
                    dve.wait_ge(s_kn, PAIRS)
                else:
                    dve.wait_ge(s_vst, 32 * m)
                for c in range(2):
                    dve.tensor_copy(VR[:, 4 * c:4 * c + 4, :], PS[:, c, :].rearrange("p (c n) -> p c n", n=P))
                dve.tensor_copy(VR[0:RS, SEQ // P, :], PS[0:RS, 2, 0:P]).then_inc(s_vr, 1)

            def k_unit(m, s, i):
                if not (isinstance(m, int) and m == 0):
                    norm(m - 1, 1 - s, C_K2)

            def v_unit(m, s, i):
                if isinstance(m, int) and m == 0:
                    norm(PAIRS - 1, 1, C_K2)
                else:
                    rows_first(m - 1)

            def q_unit(m, s, i):
                if not (isinstance(m, int) and m == 0):
                    norm(PAIRS + m - 1, 1 - s, C_Q2)

            dve.wait_ge(s_unit, U_K)
            h_split(0, C_KN)
            paired(dve, PAIRS, k_unit)
            paired(dve, PAIRS, v_unit)
            dve.memset(CUM[:, 0:1], 0.0).then_inc(s_cum, 1)
            dve.wait_ge(s_lfp, 16)
            dve.wait_ge(s_cum, 1)
            dve.tensor_tensor_scan(CUM[:, 1:], LFP[:], LFP[:], CUM[:, 0:1], ALU.add, ALU.bypass).then_inc(s_cum, 1)
            rows_first(PAIRS - 1)
            dve.wait_ge(s_unit, U_F + 1)
            dve.wait_ge(s_kst, 16 * PAIRS)
            dve.wait_ge(s_vst, 32 * PAIRS)
            h_split(KD, C_BN)
            paired(dve, PAIRS, q_unit)
            norm(2 * PAIRS - 1, 1, C_Q2)
            F, E, S, A = FL[0:H, :], SQ3[0:H, :], RS3[0:H, :], KN[0:H, :]
            dve.wait_ge(s_fl, 1)
            dve.wait_ge(s_n, 2 * PAIRS)
            dve.scalar_tensor_tensor(out=E, in0=F, scalar=-1.0, in1=F, op0=ALU.mult, op1=ALU.min).then_inc(s_f, 1)
            dve.wait_ge(s_fe, 1)
            dve.tensor_scalar(S, E, 1.0, 2.0, ALU.mult, ALU.add).then_inc(s_f, 1)
            dve.wait_ge(s_f, 2)
            dve.reciprocal(S, S).then_inc(s_f, 1)
            dve.wait_ge(s_f, 3)
            dve.tensor_tensor(E, E, S, ALU.mult).then_inc(s_f, 1)
            dve.wait_ge(s_f, 4)
            dve.tensor_tensor(S, E, E, ALU.mult).then_inc(s_f, 1)
            dve.wait_ge(s_f, 5)
            dve.wait_ge(s_kst, 32 * PAIRS)
            dve.tensor_scalar(A, S, 1.0 / 15, 0.0, ALU.mult, ALU.add).then_inc(s_f, 1)
            for j, odd in enumerate((13, 11, 9, 7, 5, 3)):
                dve.wait_ge(s_f, 6 + j)
                dve.scalar_tensor_tensor(out=A, in0=A, scalar=1.0 / odd, in1=S, op0=ALU.add,
                                         op1=ALU.mult).then_inc(s_f, 1)
            dve.wait_ge(s_f, 12)
            dve.scalar_tensor_tensor(out=A, in0=A, scalar=1.0, in1=E, op0=ALU.add, op1=ALU.mult).then_inc(s_f, 1)
            dve.wait_ge(s_f, 13)
            dve.tensor_scalar(S, F, 0.0, 1.0, ALU.min, ALU.mult).then_inc(s_f, 1)
            dve.wait_ge(s_f, 14)
            dve.scalar_tensor_tensor(out=F, in0=A, scalar=-2.0, in1=S, op0=ALU.mult, op1=ALU.add).then_inc(s_f, 1)
            dve.wait_ge(s_f, 15)
            dve.tensor_scalar(E, F, -1.0, 0.0, ALU.mult, ALU.add).then_inc(s_f, 1)
            dve.wait_ge(s_f, 16)
            for a, b in [(0, SEQ)] + [(a, a + DS) for a in range(SEQ, R, DS)]:
                t = dve.tensor_tensor_scan(A[:, a:b], E[:, a:b], E[:, a:b], CUM[0:H, 0:1], ALU.add, ALU.bypass)
            t.then_inc(s_f, 1)
            for x in range(3):
                dve.wait_ge(s_f, 17 + 2 * x)
                dve.tensor_copy(FPB[:, x, :], A).then_inc(s_f, 1)
                if x < 2:
                    dve.wait_ge(s_f, 18 + 2 * x)
                    dve.tensor_tensor(A, A, FPB[:, x, :], ALU.subtract).then_inc(s_f, 1)
            dve.wait_ge(s_cum, 2)
            dve.tensor_scalar(VRES[:], CUM[:, 1:], CUM[:, PAST:], -1.0, ALU.subtract, ALU.mult).then_inc(s_vres, 1)
            for c in range(PAST // 512):
                v = VRES[:, c * 512:(c + 1) * 512]
                o = PB[c % 2]
                if c > 1:
                    dve.wait_ge(s_pst[c % 2], 16 * (c // 2))
                for x in range(3):
                    dve.wait_ge(s_vres, 1 + 4 * c + 2 * x)
                    t = dve.tensor_copy(o[:, x, :], v)
                    t.then_inc(s_pb if x == 2 else s_vres, 1)
                    if x < 2:
                        dve.wait_ge(s_vres, 1 + 4 * c + 2 * x + 1)
                        dve.tensor_tensor(v, v, o[:, x, :], ALU.subtract).then_inc(s_vres, 1)

            def att_step(b, par, bh):
                real = not (isinstance(b, int) and b == DB)
                for t in range(16):
                    item, hl = t // 2, t % 2
                    n = P * (item + 1)
                    if real:
                        atleast(dve, s_nm, 16 * b + t - 1)
                        dve.wait_ge(s_s, 16 * b + t + 1)
                        dve.tensor_reduce(MXP[hl][:], PS[:, 2 * hl:2 * hl + 2, :].rearrange("p a n -> p (a n)")[:, 0:n],
                                          AX_X, ALU.max).then_inc(s_mx, 1)
                        dve.wait_ge(s_mx, 16 * b + t + 1)
                        atleast(dve, s_p, 16 * b + t - 1)
                        dve.tensor_scalar(NMX[hl][:], MXP[hl][:], -1.0, 0.0, ALU.mult, ALU.add).then_inc(s_nm, 1)
                    if t == 0 and started(b):
                        dve.wait_ge(s_ex, 9 * b)
                        dve.tensor_reduce(RID[:], SMD[:], AX_X, ALU.add).then_inc(s_rd, 1)
                        dve.wait_ge(s_rd, b)
                        dve.reciprocal(RID[:], RID[:]).then_inc(s_ridn, 1)
                        dve.wait_ge(s_ridn, b)
                        dve.wait_ge(s_dd, 16 * b)
                        dve.scalar_tensor_tensor(out=OD[:], in0=PS[:, 4, 0:4 * HD], scalar=RID[:], in1=M4[:],
                                                 op0=ALU.mult, op1=ALU.mult).then_inc(s_od, 1)
                        dve.wait_ge(s_od, b)
                        atleast(dve, s_to, b - 1)
                        dve.tensor_reduce(OE[:, 0:HD], OD[:].rearrange("p (g d) -> p d g", d=HD), AX_X,
                                          ALU.add).then_inc(s_oe, 1)
                        dve.wait_ge(s_oe, b)
                        dve.tensor_copy(OE[:, HD:2 * HD], OE[:, 0:HD]).then_inc(s_oe2, 1)
                    if t == NG and real:
                        dve.wait_ge(s_sc, 9 * b + NG + 1)
                        dve.tensor_reduce(MXD[:, NG:NG + 1], SC[:, PAST:PAST + RS], AX_X, ALU.max).then_inc(s_dmx, 1)
                        dve.wait_ge(s_dmx, 9 * (b + 1))
                        dve.tensor_reduce(GMD[:], MXD[:], AX_X, ALU.max).then_inc(s_gmx, 1)
                        dve.wait_ge(s_gmx, b + 1)
                        atleast(dve, s_ex, 9 * b)
                        dve.tensor_scalar(NGM[:], GMD[:], -1.0, 0.0, ALU.mult, ALU.add).then_inc(s_gm, 1)
                    if t == 0 and started(b):
                        prompt_o(b - 1, NQ - 1, 1 - par)
                        dve.wait_ge(s_to, b)
                        cols = slice(DS * b - DS, DS * b) if isinstance(b, int) else ds(DS * b - DS, DS)
                        for x in range(2):
                            src = PS[HD * x:HD * x + HD, 6, 0:P].rearrange("p (j x q) -> p j x q", x=2, q=DS)[:, :, x, :]
                            o = dve.tensor_copy(OS[HD * x:HD * x + HD, :, cols], src)
                        o.then_inc(s_os, 1)
                    if started(b):
                        half, mo = t // 8, t % 8
                        dve.wait_ge(s_ou, 16 * b - 16 + t + 1)
                        atleast(dve, s_po, 16 * b - 32 + t + 1 if not (isinstance(b, int) and b == 1) else 0)
                        x = X2[:, mo, 512 * half:512 * half + 512]
                        dve.tensor_tensor(x, PS[:, 5, :], x, ALU.add).then_inc(s_po, 1)
                    if not real:
                        continue
                    if t >= 2 and hl == 0:
                        prompt_o(b, item - 1, par)
                    if t < NG:
                        dve.wait_ge(s_sc, 9 * b + t + 1)
                        atleast(dve, s_gmx, b)
                        dve.tensor_reduce(MXD[:, t:t + 1], SC[:, 512 * t:512 * t + 512], AX_X, ALU.max).then_inc(s_dmx, 1)
                    dve.wait_ge(s_p, 16 * b + t + 1)
                    atleast(dve, s_pn, 16 * b + t - 1)
                    dve.reciprocal(RIP[hl][:], SMP[hl][:]).then_inc(s_ri, 1)
                    dve.wait_ge(s_ri, 16 * b + t + 1)
                    dve.tensor_scalar(PP[hl][:, 0:n], PP[hl][:, 0:n], RIP[hl][:], None, ALU.mult).then_inc(s_pn, 1)

            def prompt_o(b, i, par):
                dve.wait_ge(s_pv, NQ * b + i + 1)
                if i == 0:
                    dve.wait_ge(s_zp, 16 * (b + 1))
                    if not (isinstance(b, int) and b < 2):
                        dve.wait_ge(s_ou, 16 * b - 16)
                c = slice(P * i, P * i + P)
                dve.tensor_tensor(OP[par][:, c], PS[:, 7, 0:P], ZP[:, c], ALU.mult).then_inc(s_o, 1)

            dve.wait_ge(s_m4, 16)
            steps(dve, att_step)

            dve.wait_ge(s_wof, 32)
            dve.wait_ge(s_os, DB)
            dve.tensor_tensor(OS[:], OS[:], ZSM[:], ALU.mult).then_inc(s_oz, 1)
            dve.wait_ge(s_yt, 1)
            dve.wait_ge(s_po, 16 * DB)
            x = X2[:, :, SEQ:R]
            dve.tensor_tensor(x, x, PS[:, 2, :].rearrange("p (k n) -> p k n", n=RS), ALU.add).then_inc(s_y, 1)
            ple(1, U_TAIL)



def layout(x_prompt, x_sample, state_conv, cache_k, cache_v, cache_logf, page_table, p_prompt, p_sample,
           a_norm, a_w_in, a_conv_w, a_conv_b, a_ln_g, a_ln_b, a_w_out, kv_norm, kv_w, kv_k_norm, kv_f_bias,
           b_norm, b_w_q, b_q_norm, b_w_out, ple_w, ple_gate_w):
    import numpy as np

    def features_first(a):
        return a.T.reshape(a.shape[1] // P, P, a.shape[0]).transpose(1, 0, 2)

    def units(w):
        k, n = w.shape
        return w.reshape(k // P, P, n // P, P).transpose(2, 1, 0, 3).reshape(n // P, P, k)

    def columns(v):
        return v.reshape(-1, P).T

    rows = np.concatenate([x_prompt[0], x_sample.reshape(RS, D)], 0)
    prow = [np.concatenate([p_prompt[l, 0], p_sample[l].reshape(RS, PLE)], 0) for l in range(2)]
    conv = units(a_w_in[0]).reshape(3, NCH, P, D)
    conv = np.stack([conv[1], conv[0], conv[2]], 1).reshape(3 * NCH, P, D)
    wo = a_w_out[0].reshape(2, D, D)
    wo = np.stack([units(wo[0]), units(wo[1])], 1).reshape(2 * KD, P, D)
    ple = np.stack([np.concatenate([units(ple_gate_w[l]), units(ple_w[l])], 2) for l in range(2)])
    fl = np.zeros((D, P), np.float32)
    fl[:, :H] = kv_w[:, 2 * D:]
    kvq = np.concatenate([units(kv_w[:, :2 * D]), units(fl), units(b_w_q[0])], 0)
    taps = np.concatenate([a_conv_w[0], a_conv_b], 0)
    taps = taps.T.reshape(NCH, P, CW + 1)
    state = np.zeros((EA, DB, SW), np.float32)
    state[:, :, :HIST] = state_conv[0].transpose(2, 0, 1)
    fb = np.zeros((P, 1), np.float32)
    fb[:H, 0] = kv_f_bias
    twice = lambda g: np.concatenate([g, g])[:, None]
    eps = np.full((P, 1), EPS, np.float32)
    cst = np.concatenate([columns(a_norm[0]), columns(kv_norm), columns(b_norm[0]), columns(a_ln_g[0]),
                          columns(a_ln_b[0]), twice(kv_k_norm), twice(b_q_norm[0]), fb, eps, HD * eps], 1)
    ident = np.eye(P, dtype=np.float32)
    bones = np.kron(np.eye(2), np.ones((HD, HD))).astype(np.float32)
    fcon = np.stack([ident, np.ones((P, P), np.float32), bones], 1)
    bcon = np.zeros((P, B_N), np.float32)
    bcon[:, B_ID:B_ID + P] = ident
    i = np.arange(P)
    bcon[:, B_MD:B_MD + P] = np.where(i[None, :] > i[:, None], -1e30, 0)
    hq = np.arange(P)
    for part in range(3):
        bcon[32 * part + hq // DS, B_SD + hq] = 1
        for hl in range(2):
            bcon[32 * part + hl, B_SP + P * hl:B_SP + P * hl + P] = 1
    for b in range(DB):
        key = np.arange(RS)
        seen = (key[None, :] // DS == b) & (key[None, :] % DS <= hq[:, None] % DS)
        bcon[:, B_MN + RS * b:B_MN + RS * b + RS] = np.where(seen, 0, -1e30)
    for g in range(4):
        bcon[:, B_M4 + HD * g:B_M4 + HD * g + HD] = (hq[:, None] // DS % 4 == g)
    c = np.ascontiguousarray
    return {
        "xT": c(features_first(rows)), "pT": c(np.stack([features_first(p) for p in prow])),
        "wA": c(conv), "wO": c(wo), "wP": c(ple), "wB": c(kvq), "wW": c(b_w_out[0].reshape(PAIRS, P, D)),
        "cw": c(taps), "est": c(state.reshape(NCH, P, DB * SW)), "cst": c(cst), "fcon": c(fcon), "bcon": bcon,
        "ck": c(cache_k.reshape(-1, PAGE, PAIRS, P).transpose(0, 3, 2, 1)).reshape(-1, P, D),
        "cv": c(cache_v.reshape(-1, PAGE, D)), "clf": c(cache_logf.transpose(0, 2, 1)),
        "ptab": c(page_table.reshape(1, DB * NPG)),
    }


_OUTS = [("yT", (P, KD, R)), ("cpT", (NCH, P, HIST)), ("csT", (NCH, P, DB * SW)), ("kT", (PAIRS, P, R)),
         ("vR", (R, D)), ("lfT", (H, R))]


def kernel(**inputs):
    import numpy as np
    import concourse.bacc as bacc
    from concourse.bass_utils import run_bass_kernel_spmd as run

    arrays = layout(**{k: np.asarray(v) for k, v in inputs.items()})
    nc = bacc.Bacc("TRN2", target_bir_lowering=False, num_devices=1)
    args = [nc.dram_tensor(n, a.shape, mybir.dt.from_np(a.dtype), kind="ExternalInput").ap()
            for n, a in arrays.items()]
    args += [nc.dram_tensor(n, s, F32, kind="ExternalOutput").ap() for n, s in _OUTS]
    build(nc, *args)
    got = run(nc, [arrays], core_ids=[0]).results[0]
    y = got["yT"].transpose(2, 1, 0).reshape(R, D)
    conv_p = got["cpT"].transpose(2, 0, 1).reshape(1, 1, HIST, EA)
    conv_s = got["csT"].reshape(NCH, P, DB, SW)[..., DS:].transpose(2, 3, 0, 1).reshape(1, DB, HIST, EA)
    k = got["kT"].transpose(2, 0, 1).reshape(R, H, HD)
    v = got["vR"].reshape(R, H, HD)
    lf = got["lfT"].T
    c = np.ascontiguousarray
    return (c(y[:SEQ]).reshape(1, SEQ, D), c(y[SEQ:]).reshape(DB, DS, D), c(conv_p),
            c(k[:SEQ])[None], c(v[:SEQ])[None], c(lf[:SEQ])[None], c(conv_s),
            c(k[SEQ:]).reshape(DB, DS, H, HD), c(v[SEQ:]).reshape(DB, DS, H, HD), c(lf[SEQ:]).reshape(DB, DS, H))
```

```python
from contextlib import ExitStack

import concourse.bass as bass
from concourse import mybir

F32 = mybir.dt.float32
F32R = mybir.dt.float32r
BF16 = mybir.dt.bfloat16
I32 = mybir.dt.int32
ALU = mybir.AluOpType
ACT = mybir.ActivationFunctionType
AX_X = mybir.AxisListType.X
ds = bass.ds

P = 128
D = 1024
KD = D // P
SEQ = 1024
DB, DS = 8, 8
RS = DB * DS
R = SEQ + RS
RCH = [(0, 384), (384, 768), (768, R)]
EA = 2 * D
NCH = EA // P
CW = 31
HIST = CW - 1
H, HD = 16, 64
PAIRS = H // 2
PLE = 256
EPS = 1e-6
PAST, PAGE = 4096, 128
NPG = PAST // PAGE
GP = 4
NG = NPG // GP
NQ = SEQ // P
USAMP = HIST + SEQ
SW = HIST + DS
UEXT = USAMP + DB * SW
NT = 9
NV = CW - NT
SLOT = 10 * P
U_CONV, U_OUT, U_PLE, U_K, U_V, U_F, U_Q, U_Z, U_TAIL = 0, 48, 64, 72, 80, 88, 89, 97, 105
F_STEPS = 22
C_AN, C_KN, C_BN, C_LG, C_LB, C_K2, C_Q2, C_FB, C_EPS, C_EPQ, C_N = 0, 8, 16, 24, 40, 56, 57, 58, 59, 60, 61
B_ID, B_MD, B_SD, B_SP, B_MN, B_BF, B_M4, B_N = 0, 128, 256, 384, 640, 1152, 1152, 1408
TILE = 4352


def atleast(eng, sem, value):
    if not isinstance(value, int) or value > 0:
        eng.wait_ge(sem, value)


def flat(ap):
    return ap.rearrange("p a n -> p (a n)")


def build(nc, xT, pT, wA, wO, wP, wB, wW, cw, est, cst, fcon, bcon, ck, cv, clf, ptab,
          yT, cpT, csT, kT, vR, lfT):
    zT = nc.dram_tensor("zT_scr", (NCH, P, R), F32, kind="Internal").ap()
    qT = nc.dram_tensor("qT_scr", (PAIRS, P, R), F32, kind="Internal").ap()
    gT = nc.dram_tensor("gT_scr", (PAIRS, P, R), F32, kind="Internal").ap()
    lfG = nc.dram_tensor("lfG_scr", (DB * H, PAST), F32, kind="Internal").ap()
    cPr = nc.dram_tensor("cPr_scr", (3, H, SEQ), BF16, kind="Internal").ap()
    cPa = nc.dram_tensor("cPa_scr", (3, DB * H, PAST), BF16, kind="Internal").ap()
    cNw = nc.dram_tensor("cNw_scr", (3, H, RS), BF16, kind="Internal").ap()
    with ExitStack() as ctx:
        sbuf_base = (nc.sbuf_base + 31) // 32 * 32
        sbuf_end = nc.sbuf_usable_end

        class Map:
            def __init__(self, at):
                self.at = at

            def __call__(self, name, shape, dt=F32):
                n = 2 if dt == BF16 else 4
                for s in shape[1:]:
                    n *= s
                t = nc.alloc_sbuf_tensor_at(name, shape, dt, offset=self.at)
                self.at += (n + 31) // 32 * 32
                assert self.at <= sbuf_end, (name, self.at, sbuf_end)
                return t

        def sem(name):
            return ctx.enter_context(nc.semaphore(name))

        PS = ctx.enter_context(nc.psum_tensor("PS", [P, 8, 512], F32))

        m = Map(sbuf_base)
        CST = m("CST", [P, C_N])
        FCON = m("FCON", [P, 3, P])
        IDENT, ONES, BONES = FCON[:, 0, :], FCON[:, 1, :], FCON[:, 2, :]
        PTAB = m("PTAB", [1, DB * NPG], I32)
        at_x = m.at
        UX = [m(f"UX{s}", [P, UEXT]) for s in range(2)]
        ZS = m("ZS", [P, R])
        PROD = [m(f"PROD{s}", [P, R]) for s in range(2)]
        ACC = m("ACC", [P, R])
        CSUM = m("CSUM", [P, R])
        CHAIN = m("CHAIN", [P, R])
        CWT = [m(f"CWT{s}", [P, CW + 1]) for s in range(2)]
        at_h = m.at
        HH = m("HH", [P, KD, R], F32R)
        HL = m("HL", [P, KD, R], F32R)
        at_c = m.at
        CC = m("CC", [P, NCH, R])
        at_r = m.at
        RAW = [m(f"RAW{s}", [P, SLOT]) for s in range(2)]
        WH = [m(f"WH{s}", [P, SLOT], F32R) for s in range(2)]
        WL = [m(f"WL{s}", [P, SLOT], F32R) for s in range(2)]
        XIN = Map(at_c)("XIN", [P, KD, R])
        m = Map(at_x)
        T0 = [m(f"T0{s}", [P, R]) for s in range(2)]
        RSTD0 = m("RSTD0", [P, R])
        m = Map(at_x)
        MU = m("MU", [P, R])
        T1 = [m(f"T1{s}", [P, R]) for s in range(2)]
        Y1 = [m(f"Y1{s}", [P, R]) for s in range(3)]
        Z1 = [m(f"Z1{s}", [P, R]) for s in range(2)]
        assert m.at <= at_h
        SQ1 = T1 + Y1[0:2]
        MH = Map(at_h)("MH", [P, NCH, R], F32R)
        ML = Map(at_c)("ML", [P, NCH, R], F32R)
        X2 = Map(at_x)("X2", [P, KD, R])
        m = Map(at_h)
        XH = m("XH", [P, KD, R], F32R)
        XL = m("XL", [P, KD, R], F32R)
        m = Map(at_c)
        RSTD2 = m("RSTD2", [P, R])
        PR = m("PR", [P, 2, R])
        PH = m("PH", [P, 2, R], F32R)
        PL = m("PL", [P, 2, R], F32R)
        SG = m("SG", [P, R])
        T2 = m("T2", [P, R])
        SQ2 = m("SQ2", [P, R])
        SS2 = m("SS2", [P, R])
        m = Map(at_h)
        GH = m("GH", [P, KD, R], F32R)
        GL = m("GL", [P, KD, R], F32R)
        m = Map(at_c + TILE)
        KC = [m(f"KC{s}", [P, R]) for s in range(2)]
        SQ3 = m("SQ3", [P, R])
        RS3 = m("RS3", [P, R])
        KN = m("KN", [P, R])
        FL = m("FL", [P, R])
        LFP = m("LFP", [P, PAST])
        CUM = m("CUM", [P, 1 + PAST])
        PB = [m(f"PB{s}", [P, 3, 512], BF16) for s in range(2)]
        assert m.at <= at_r
        VR = Map(at_c + 3 * TILE)("VR", [P, R // P + 1, P])
        VRES = LFP
        FPB = Map(at_c + 3 * TILE)("FPB", [H, 3, R], BF16)

        m = Map(at_x + KD * R * 4)
        NMX = [m(f"NMX{s}", [P, 1]) for s in range(2)]
        MXP = [m(f"MXP{s}", [P, 1]) for s in range(2)]
        SMP = [m(f"SMP{s}", [P, 1]) for s in range(2)]
        RIP = [m(f"RIP{s}", [P, 1]) for s in range(2)]
        MXD = m("MXD", [P, NG + 1])
        SMD = m("SMD", [P, NG + 1])
        GMD, NGM, RID = m("GMD", [P, 1]), m("NGM", [P, 1]), m("RID", [P, 1])
        QD = m("QD", [P, PAIRS, 32])
        OE = m("OE", [P, 2 * HD])
        assert m.at <= at_h
        m = Map(at_h)
        KV = [m(f"KV{s}", [P, GP, D]) for s in range(4)]
        PP = [m("PP0", [P, SEQ])]
        m = Map(at_c)
        SC = m("SC", [P, PAST + P])
        PT = [m(f"PT{s}", [P, SEQ]) for s in range(2)]
        PP.append(m("PP1", [P, SEQ]))
        OD = m("OD", [P, 4 * HD])
        assert m.at <= at_c + 7 * TILE
        m = Map(at_c + 7 * TILE)
        CB = m("CB", [96, PAST + RS], BF16)
        CP = [m(f"CP{s}", [96, SEQ], BF16) for s in range(2)]
        BCON = m("BCON", [P, B_BF], BF16)
        M4 = m("M4", [P, B_N - B_M4])
        KNW = m("KNW", [P, PAIRS, RS])
        VNW = m("VNW", [RS, D])
        BRAW = Map(m.at)("BRAW", [P, B_BF])
        KT = [m("KT0", [P, SEQ])]
        QT = [m("QT0", [P, SEQ])]
        VP = m("VP", [P, NQ, P])
        ZP = m("ZP", [P, SEQ])
        PTN = m("PTN", [RS, P])
        assert m.at <= at_r
        m = Map(at_r)
        KT.append(m("KT1", [P, SEQ]))
        QT.append(m("QT1", [P, SEQ]))
        OP = [m(f"OP{s}", [P, SEQ]) for s in range(2)]
        WOP = [m(f"WOP{s}", [P, D]) for s in range(2)]
        PTD = [m(f"PTD{s}", [P, GP, P]) for s in range(2)]
        OS = m("OS", [P, PAIRS, RS])
        m = Map(at_c + 9 * TILE)
        WOF = [m(f"WOF{p}", [P, D]) for p in range(PAIRS - 1)]
        assert m.at <= at_r
        WOF.append(Map(at_c)("WOF7", [P, D]))
        YS = Map(at_c + 7 * TILE)("YS", [RS, D])
        ZSM = Map(at_c + 8 * TILE)("ZSM", [P, PAIRS, RS])

        s_con, s_pt = sem("con_in"), sem("ptab_in")
        s_xin = [sem(f"xin{k}") for k in range(KD)]
        s_raw = [sem(f"raw_in{s}") for s in range(2)]
        s_hi, s_lo, s_unit = sem("whi"), sem("wlo"), sem("unit_done")
        s_sq0, s_st0, s_sd0, s_rc0 = sem("sq0"), sem("stat0"), sem("sd0"), sem("rstd0")
        s_t0, s_hh, s_h = sem("h_f32"), sem("h_hi"), sem("h_lo")
        s_est = [sem(f"est_in{s}") for s in range(2)]
        s_pad, s_sg, s_u, s_zs, s_zst, s_cst = (sem(x) for x in ("pad", "sigb", "u", "zs", "z_out", "state_out"))
        s_prod, s_add, s_tap, s_c, s_csum = (sem(x) for x in ("prod", "add", "tap", "conv", "csum"))
        s_mmu, s_mu, s_xc, s_sq1, s_var, s_sd1, s_rc1 = (
            sem(x) for x in ("mu_mm", "mu", "xc", "sq1", "var_mm", "sd1", "rstd1"))
        s_sqp = sem("sq1_pairs")
        s_t1, s_y1, s_m, s_mh, s_ml = (sem(x) for x in ("lnx", "lny", "m_f32", "m_hi", "m_lo"))
        s_z1 = [sem(f"z_in{s}") for s in range(2)]
        s_x1in, s_x1 = sem("x_in2"), sem("x1")
        s_xh, s_xl, s_prin, s_ph, s_pl = (sem(x) for x in ("x_hi", "x_lo", "p_in", "p_hi", "p_lo"))
        s_gate, s_sgp, s_t2, s_x2, s_sq2, s_ss2, s_st2, s_sd2, s_rc2 = (
            sem(x) for x in ("gate_mm", "gate_sig", "ple_prod", "x2", "sq2", "sumsq2", "stat2", "sd2", "rstd2"))
        s_g, s_gh, s_gl = sem("hkv_f32"), sem("hkv_hi"), sem("hkv_lo")
        s_kc, s_sq3, s_n, s_rs, s_rc, s_kn, s_kst = (
            sem(x) for x in ("kvq_copy", "sq3", "norm_mm", "norm_sd", "norm_rstd", "normed", "kq_out"))
        s_tr, s_vr, s_vst, s_zc = (sem(x) for x in ("v_transposed", "v_rows", "v_out", "z_silu"))
        s_gst = [sem(f"g_out{s}") for s in range(2)]
        s_fl, s_f, s_fe, s_fst = (sem(x) for x in ("fl", "logf_step", "logf_exp", "logf_out"))
        s_lfg, s_lfp, s_cum, s_pb, s_vres = (sem(x) for x in ("past_logf_gathered", "past_logf_in", "past_cum", "past_parts", "past_residual"))
        s_pst = [sem(f"past_out{s}") for s in range(2)]
        s_q, s_wo = [sem(f"kq_in{s}") for s in range(2)], [sem(f"wo_in{s}") for s in range(2)]
        s_kv = [sem(f"pages_in{s}") for s in range(4)]
        s_pad2, s_bcon, s_knw, s_qd, s_cb, s_vp, s_zp = (
            sem(x) for x in ("pads", "bias_con", "new_kv_in", "qd_in", "cb_in", "v_in", "z_in"))
        s_s, s_mx, s_nm, s_p, s_ri, s_pn, s_trp, s_ev, s_pv, s_o, s_ou, s_po = (
            sem(x) for x in ("scores", "row_max", "neg_max", "exp", "rinv", "probs", "p_transposed", "pt",
                             "pv", "o", "out_mm", "out_added"))
        s_dd, s_qn, s_sc, s_dmx, s_gmx, s_gm, s_ex, s_td, s_dv, s_rd, s_ridn, s_od, s_oe, s_oe2, s_to, s_os = (
            sem(x) for x in ("pages_used", "new_scores", "sc_copied", "group_max", "dec_max", "dec_neg_max", "dec_exp",
                             "d_transposed", "ptd", "dec_sum", "dec_rinv", "dec_o", "dec_o_heads", "dec_o_dup",
                             "dec_o_t", "dec_o_done"))
        s_zsm = sem("silu_z_in")
        s_wof, s_oz, s_ys, s_yc, s_yt, s_y = (
            sem(x) for x in ("wof_in", "oz", "ys_mm", "ys", "ys_t", "x3"))
        s_zero, s_braw, s_m4, s_end = sem("zero"), sem("braw_in"), sem("m4_in"), sem("y_out")

        block = ctx.enter_context(nc.Block())

        def paired(eng, n, body):
            for i in (0, 1):
                body(i, i, 0)
            with eng.Fori(1, n // 2 - 1) as i:
                body(2 * i, 0, i)
                body(2 * i + 1, 1, i)
            for i in (n - 2, n - 1):
                body(i, i % 2, i // 2)

        def at(t, i):
            return t[i] if isinstance(i, int) else t[ds(i, 1)].rearrange("x a b -> (x a) b")

        def tile(t, i):
            return t[:, i, :] if isinstance(i, int) else flat(t[:, ds(i, 1), :])

        def decode_rows(t):
            return t[:, SEQ:R].rearrange("p (b t) -> p b t", t=DS)

        def decode_window(ux, j):
            return ux[:, USAMP:UEXT].rearrange("p (b w) -> p b w", w=SW)[:, :, j:j + DS]

        def u_place(ux, r):
            a, b = RCH[r]
            if b <= SEQ:
                return [(ux[:, HIST + a:HIST + b], 0, b - a, False)]
            return [(ux[:, HIST + a:HIST + SEQ], 0, SEQ - a, False),
                    (decode_window(ux, HIST), SEQ - a, R - a, True)]

        def bank(st, r):
            return PS[:, 3 * st + r, :]

        def rows3(ap):
            return ap.rearrange("p (b t) -> p b t", t=DS)

        order = (0, 7, 1, 6, 2, 5, 3, 4)

        def evacs(b, t, c=None):
            if t < 0:
                b, t = b - 1, t + 16
            before = sum(1 + (order[x // 2] >= 4) for x in range(t))
            return 24 * b + before + 1 + ((order[t // 2] >= 4) if c is None else c)

        def started(b):
            return not (isinstance(b, int) and b == 0)

        def steps(eng, body):
            body(0, 0, 0)
            body(1, 1, 0)
            with eng.Fori(1, DB // 2) as i:
                body(2 * i, 0, i)
                body(2 * i + 1, 1, i)
            body(DB, 0, DB // 2)

        @block.sync
        def _(sp):
            def raw(u, src, s, n=KD * P):
                atleast(sp, s_lo, u - 1)
                sp.dma_start(RAW[s][:, 0:n], src).then_inc(s_raw[s], 16)

            for k in range(KD):
                sp.dma_start(XIN[:, k, :], xT[:, k, :]).then_inc(s_xin[k], 16)
                if k == 0:
                    sp.dma_start(CST[:], cst).then_inc(s_con, 16)
                    sp.dma_start(FCON[:], fcon).then_inc(s_con, 16)
                    sp.dma_start(PTAB[:], ptab).then_inc(s_pt, 16)
            raw(0, wA[0], 0)
            raw(1, wA[1], 1)
            sp.wait_ge(s_h, KD)
            for arr, dst in ((est, UX[0][:, USAMP:UEXT]), (cw, CWT[0][:])):
                sp.dma_start(dst, arr[0]).then_inc(s_est[0], 16)
            for u in (2, 3, 4):
                raw(u, wA[u], u % 2)

            def past_logf(b, first, n):
                with sp.Fori(first, first + n) as j:
                    page = sp.value_load(PTAB[0:1, ds(NPG * b + j, 1)], min_val=0, max_val=clf.shape[0] - 1)
                    sp.dma_start(lfG[ds(H * b, H), ds(j * PAGE, PAGE)], at(clf, page)).then_inc(s_lfg, 16)

            sp.wait_ge(s_pt, 16)

            def chunk(n, s, i):
                sp.wait_ge(s_u, n + 1)
                sp.dma_start(at(cpT, n), UX[s][:, USAMP - HIST:USAMP]).then_inc(s_cst, 16)
                sp.dma_start(at(csT, n), UX[s][:, USAMP:UEXT]).then_inc(s_cst, 16)
                if not (isinstance(n, int) and n == NCH - 1):
                    atleast(sp, s_cst, 32 * n)
                    atleast(sp, s_c, n)
                    sp.dma_start(UX[1 - s][:, USAMP:UEXT], at(est, n + 1)).then_inc(s_est[1 - s], 16)
                    sp.dma_start(CWT[1 - s][:], at(cw, n + 1)).then_inc(s_est[1 - s], 16)
                for j in (5, 6, 7):
                    u = 3 * n + j
                    if isinstance(u, int) and u == U_OUT + 4:
                        past_logf(i, NPG // 2 * s + 10, 6)
                        break
                    if isinstance(u, int) and u >= U_OUT:
                        raw(u, wO[u - U_OUT], (s + j) % 2)
                    else:
                        raw(u, at(wA, u), (s + j) % 2)
                    past_logf(i, NPG // 2 * s + 5 * (j - 5), 6 if j == 7 else 5)

            paired(sp, NCH, chunk)
            sp.wait_ge(s_zst, 16 * NCH)
            sp.wait_ge(s_mu, 1)
            for n in range(NCH):
                atleast(sp, s_m, n - 1)
                sp.dma_start(Z1[n % 2][:], zT[n]).then_inc(s_z1[n % 2], 16)
            sp.wait_ge(s_ml, NCH)
            sp.dma_start(X2[:], xT).then_inc(s_x1in, 16)
            for u in range(U_OUT + 4, U_PLE):
                raw(u, wO[u - U_OUT], u % 2)
            def ple_loads(l, u0):
                with sp.Fori(0, KD // 2) as i:
                    for s in range(2):
                        raw(u0 + 2 * i + s, at(wP[l], 2 * i + s), (u0 + s) % 2, SLOT)

            ple_loads(0, U_PLE)
            for u in range(U_K, U_K + 2):
                raw(u, wB[u - U_K], u % 2)
            sp.wait_ge(s_lfg, 16 * NPG * DB)
            sp.wait_ge(s_sd2, 1)
            sp.dma_start(LFP[:], lfG).then_inc(s_lfp, 16)
            with sp.Fori(1, 16) as i:
                for s in range(2):
                    raw(U_K + 2 * i + s, at(wB, 2 * i + s), s)
            raw(U_TAIL - 1, wB[U_TAIL - 1 - U_K], 0)

            sp.wait_ge(s_unit, U_TAIL)

            def pages(b):
                for t in range(16):
                    for kk in range(GP):
                        page = sp.value_load(PTAB[0:1, ds(NPG * b + GP * (t % NG) + kk, 1)], min_val=0,
                                             max_val=ck.shape[0] - 1)
                        if kk == 0 and (started(b) or t >= 4):
                            sp.wait_ge(s_dd, 16 * b + t - 3)
                        sp.dma_start(KV[t % 4][:, kk, :], at(ck if t < NG else cv, page)).then_inc(s_kv[t % 4], 16)

            pages(0)
            with sp.Fori(1, DB) as b:
                pages(b)
            sp.wait_ge(s_ou, 16 * DB - 15)
            ple_loads(1, U_TAIL)
            for m in range(KD):
                sp.wait_ge(s_x2, KD + m + 1)
                sp.dma_start(yT[:, m, :], X2[:, m, :]).then_inc(s_end, 16)
            sp.wait_ge(s_end, 16 * KD)


        def group(pe, st, s, xh, xl, nk, ready=None, first=True, last=True, off=0, base=0):
            for k in range(nk):
                if ready is not None:
                    pe.wait_ge(ready, base + k + 1 if first else nk + k + 1)
                kk = slice((off + k) * P, (off + k + 1) * P)
                for r, (a, b) in enumerate(RCH):
                    out = bank(st, r)[:, 0:b - a]
                    pe.matmul(out, WH[s][:, kk], xh[:, k, a:b], start=first and k == 0, stop=False)
                    pe.matmul(out, WH[s][:, kk], xl[:, k, a:b], start=False, stop=False)
                    mm = pe.matmul(out, WL[s][:, kk], xh[:, k, a:b], start=False, stop=last and k == nk - 1)
            return mm

        def colsum(pe, st, src, first=True, last=True, w=None):
            for r, (a, b) in enumerate(RCH):
                mm = pe.matmul(bank(st, r)[:, 0:b - a], ONES if w is None else w, src[:, a:b], start=first, stop=last)
            return mm

        @block.tensor
        def _(pe):
            pe.wait_ge(s_con, 32)
            for k in range(KD):
                pe.wait_ge(s_sq0, k + 1)
                colsum(pe, 1, T0[k % 2], k == 0, k == KD - 1).then_inc(s_st0, 1)

            def chunk(n, s, i):
                for kind, (free, v) in enumerate(((s_u, n), (s_zs, n), (s_sg, n + 1))):
                    pe.wait_ge(s_lo, 3 * n + kind + 1)
                    atleast(pe, free, v)
                    if isinstance(n, int) and n == 0 and kind == 1:
                        pe.wait_ge(s_sd0, 1)
                    group(pe, (s + kind) % 2, (s + kind) % 2, HH, HL, KD,
                          ready=s_h if isinstance(n, int) and n == 0 and kind == 0 else None).then_inc(s_unit, 1)

            paired(pe, NCH, chunk)
            pe.wait_ge(s_csum, NCH + 1)
            pe.wait_ge(s_u, NCH)
            colsum(pe, 0, CSUM).then_inc(s_mmu, 1)
            pe.wait_ge(s_zs, NCH)
            for p in range(NCH // 2):
                pe.wait_ge(s_sqp, p + 1)
                colsum(pe, 1, SQ1[2 * (p % 2)], p == 0, p == NCH // 2 - 1).then_inc(s_var, 1)

            def out0(m, st, ready=None):
                for half in range(2):
                    u = U_OUT + 2 * m + half
                    pe.wait_ge(s_lo, u + 1)
                    if half == 0:
                        if isinstance(m, int) and m < 2:
                            pe.wait_ge((s_mu, s_sd1)[m], 1)
                        else:
                            pe.wait_ge(s_x1, m - 1)
                    group(pe, st, half, MH[:, KD * half:KD * half + KD, :], ML[:, KD * half:KD * half + KD, :], KD,
                          ready=ready, first=half == 0, last=half == 1).then_inc(s_unit, 1)

            out0(0, 0, s_ml)
            out0(1, 1)
            with pe.Fori(1, 4) as i:
                out0(2 * i, 0)
                out0(2 * i + 1, 1)
            def ple(l, u0, free_gate, free_p):
                def unit(m, s, i):
                    first = isinstance(m, int) and m == 0
                    pe.wait_ge(s_lo, u0 + m + 1)
                    pe.wait_ge(*(free_gate if first else (s_sgp, KD * l + m)))
                    group(pe, 0, (u0 + s) % 2, XH, XL, KD, ready=s_xl if first and l == 0 else None,
                          base=KD * l).then_inc(s_gate, 1)
                    pe.wait_ge(*(free_p if first else (s_t2, KD * l + m)))
                    group(pe, 1, (u0 + s) % 2, PH, PL, 2, ready=s_pl if first else None, base=2 * l,
                          off=KD).then_inc(s_unit, 1)
                paired(pe, KD, unit)

            ple(0, U_PLE, (s_x1, KD - 1), (s_x1, KD))

            def main(u, s, st=1, ready=None, base=0):
                pe.wait_ge(s_lo, u + 1)
                group(pe, st, s, GH, GL, KD, ready=ready, base=base).then_inc(s_unit, 1)

            def norm(p):
                pe.wait_ge(s_sq3, p + 1)
                atleast(pe, s_rs, p)
                colsum(pe, 0, SQ3, w=BONES).then_inc(s_n, 1)

            def transposes(m, s):
                if isinstance(m, int) and m == 0:
                    pe.wait_ge(s_rs, PAIRS)
                else:
                    pe.wait_ge(s_vr, m)
                pe.wait_ge(s_kc, PAIRS + m + 1)
                for c in range((R + P - 1) // P):
                    n = min(P, R - c * P)
                    t = pe.transpose(PS[0:n, c // 4, (c % 4) * P:(c % 4 + 1) * P], KC[s][:, c * P:c * P + n], IDENT)
                t.then_inc(s_tr, 1)

            pe.wait_ge(s_ss2, KD + 1)
            pe.wait_ge(s_sgp, KD)
            colsum(pe, 0, SS2).then_inc(s_st2, 1)

            def k_unit(m, s, i):
                first = isinstance(m, int) and m == 0
                pe.wait_ge(*((s_t2, KD) if first else (s_kc, m)))
                main(U_K + m, s, ready=s_gl if first else None)
                if not first:
                    norm(m - 1)

            def v_unit(m, s, i):
                pe.wait_ge(s_kc, PAIRS + m)
                main(U_V + m, s)
                if isinstance(m, int) and m == 0:
                    norm(PAIRS - 1)
                else:
                    transposes(m - 1, 1 - s)

            def q_unit(m, s, i):
                first = isinstance(m, int) and m == 0
                pe.wait_ge(*((s_fl, 1) if first else (s_kc, 2 * PAIRS + m)))
                main(U_Q + m, 1 - s, ready=s_gl if first else None, base=KD)
                if not first:
                    norm(PAIRS + m - 1)

            def z_unit(m, s, i):
                if isinstance(m, int) and m < 2:
                    pe.wait_ge(*((s_kc, 3 * PAIRS), (s_rs, 2 * PAIRS))[m])
                else:
                    pe.wait_ge(s_zc, m - 1)
                main(U_Z + m, 1 - s, st=1 - s)
                if isinstance(m, int) and m == 0:
                    norm(2 * PAIRS - 1)

            paired(pe, PAIRS, k_unit)
            paired(pe, PAIRS, v_unit)
            pe.wait_ge(s_kc, 2 * PAIRS)
            main(U_F, 0)
            transposes(PAIRS - 1, 1)
            paired(pe, PAIRS, q_unit)
            paired(pe, PAIRS, z_unit)

            def att_step(b, par, bh):
                real = not (isinstance(b, int) and b == DB)
                for t in range(16 if real else 1):
                    if real and t > NG:
                        decode_transpose(b, t - NG)
                    if real:
                        scores(b, t, par, bh)
                    if started(b) or t > 0:
                        prompt_transpose(b, t)
                    if t == 0 and started(b):
                        prompt_pv(b - 1, NQ - 1)
                    if real and t < NG:
                        decode_scores(b, t)
                    if t == 0 and started(b):
                        pe.wait_ge(s_oe2, b)
                        pe.wait_ge(s_ev, evacs(b, -1))
                        pe.transpose(PS[:, 6, 0:P], OE[:], IDENT).then_inc(s_to, 1)
                    if real and t > NG:
                        decode_pv(b, t)
                    if started(b) and real:
                        out_product(b, t, par, bh)
                    if real and t >= 2 and t % 2 == 0:
                        prompt_pv(b, t // 2 - 1)
                    if real and t == NG - 1:
                        new_scores(b)
                    if real and t == NG:
                        pe.wait_ge(s_ex, 9 * b + 1)
                        atleast(pe, s_os, b)
                        pe.wait_ge(s_ev, evacs(b, t - 1))
                        pe.transpose(PS[:, 6, 0:P], SC[:, PAST:PAST + P], IDENT).then_inc(s_td, 1)
                        decode_transpose(b, 0)
                        decode_pv(b, t)

            def scores(b, t, par, bh):
                item, hl = order[t // 2], t % 2
                n = P * (item + 1)
                if t == 0:
                    pe.wait_ge(s_q[par], 80 * (bh + 1))
                atleast(pe, s_p, 16 * b + t - 1)
                for c in range((n + 511) // 512):
                    a, e = 512 * c, min(n, 512 * c + 512)
                    out = PS[:, 2 * hl + c, :]
                    pe.matmul(out[:, 0:e - a], BCON[0:96, B_SP + P * hl:B_SP + P * hl + P], CP[par][:, a:e],
                              start=True, stop=False)
                    if e == n:
                        pe.matmul(out[:, n - P - a:n - a], BCON[:, B_ID:B_ID + P], BCON[:, B_MD:B_MD + P],
                                  start=False, stop=False)
                    mm = pe.matmul(out[:, 0:e - a], QT[par][HD * hl:HD * hl + HD, P * item:P * item + P],
                                   KT[par][HD * hl:HD * hl + HD, a:e], start=False, stop=True)
                mm.then_inc(s_s, 1)

            def prompt_transpose(b, t):
                tp = (t - 1) % 16
                pe.wait_ge(s_pn, 16 * b + t)
                nb = order[tp // 2] + 1
                for c in range((nb + 3) // 4):
                    if c == 0:
                        if started(b) or t > 1:
                            pe.wait_ge(s_ev, evacs(b, t - 2, 0))
                        if started(b):
                            atleast(pe, s_po, 16 * b - 16 + t)
                    else:
                        if started(b) or t > 1:
                            pe.wait_ge(s_ev, evacs(b, t - 2))
                        atleast(pe, s_dv, 9 * b + max(0, t - NG + 2 if t > NG else 0))
                        atleast(pe, s_os, b if t else b - 1)
                    for k in range(4 * c, min(nb, 4 * c + 4)):
                        mm = pe.transpose(PS[:, 5 + c, P * (k % 4):P * (k % 4) + P],
                                          PP[tp % 2][:, P * k:P * k + P], IDENT)
                    mm.then_inc(s_trp, 1)

            def decode_scores(b, t):
                if t == 0:
                    atleast(pe, s_od, b)
                    pe.wait_ge(s_qd, 64 * (b + 1))
                    pe.wait_ge(s_cb, 48 * (b + 1) + 48)
                else:
                    pe.wait_ge(s_sc, 9 * b + t)
                pe.wait_ge(s_kv[t % 4], 64 * (4 * b + t // 4 + 1))
                pe.matmul(PS[:, 4, :], BCON[0:96, B_SD:B_SD + P], CB[:, 512 * t:512 * t + 512], start=True, stop=False)
                for x in range(2):
                    for j in range(4):
                        p = 2 * j + x
                        mm = pe.matmul(PS[32 * j:32 * j + 32, 4, :], QD[:, p, :], KV[t % 4][:, :, P * p:P * p + P],
                                       start=False, stop=x == 1)
                mm.then_inc(s_dd, 1)

            def new_scores(b):
                pe.wait_ge(s_sc, 9 * b + NG)
                out = PS[:, 4, 0:RS]
                pe.matmul(out, BCON[0:96, B_SD:B_SD + P], CB[:, PAST:PAST + RS], start=True, stop=False)
                mn = slice(B_MN + RS * b, B_MN + RS * b + RS) if isinstance(b, int) else ds(B_MN + RS * b, RS)
                pe.matmul(out, BCON[:, B_ID:B_ID + P], BCON[:, mn], start=False, stop=False)
                for x in range(2):
                    for j in range(4):
                        p = 2 * j + x
                        mm = pe.matmul(PS[32 * j:32 * j + 32, 4, 0:RS], QD[:, p, :], KNW[:, p, :],
                                       start=False, stop=x == 1)
                mm.then_inc(s_qn, 1)

            def out_product(b, t, par, bh):
                half, mo = t // 8, t % 8
                pe.wait_ge(s_ev, evacs(b, t - 1, 0))
                atleast(pe, s_po, 16 * b - 16 + t)
                if t == 0:
                    pe.wait_ge(s_wo[1 - par], 16 * (bh + par))
                    pe.wait_ge(s_o, NQ * b - 1)
                if t == 8:
                    pe.wait_ge(s_o, NQ * b)
                pe.matmul(PS[:, 5, :], WOP[1 - par][:, P * mo:P * mo + P],
                          OP[1 - par][:, 512 * half:512 * half + 512], start=True, stop=True).then_inc(s_ou, 1)

            def decode_transpose(b, j):
                pe.wait_ge(s_ex, 9 * b + j + 2)
                pe.wait_ge(s_dv, 9 * b + j + 1)
                pe.wait_ge(s_ev, evacs(b, NG + j - (2 if j else 1)))
                for kk in range(GP):
                    mm = pe.transpose(PS[:, 6, P * kk:P * kk + P], SC[:, 512 * j + P * kk:512 * j + P * kk + P], IDENT)
                mm.then_inc(s_td, 1)

            def decode_pv(b, t):
                j = t - NG
                if j == 0:
                    pe.wait_ge(s_sc, 9 * b + NG + 1)
                pe.wait_ge(s_dv, 9 * b + j + 2)
                pe.wait_ge(s_kv[t % 4], 64 * (4 * b + t // 4 + 1))
                for kk in range(GP):
                    for g in range(4):
                        mm = pe.matmul(PS[32 * g:32 * g + 32, 4, 0:4 * HD], PTD[j % 2][:, kk, 32 * g:32 * g + 32],
                                       KV[t % 4][:, kk, 4 * HD * g:4 * HD * g + 4 * HD], start=j == 0 and kk == 0,
                                       stop=j == NG - 1 and kk == GP - 1)
                    if j == kk == 0:
                        for g in range(4):
                            pe.matmul(PS[32 * g:32 * g + 32, 4, 0:4 * HD], PTN[:, 32 * g:32 * g + 32],
                                      VNW[:, 4 * HD * g:4 * HD * g + 4 * HD], start=False, stop=False)
                mm.then_inc(s_dd, 1)

            def prompt_pv(b, i):
                pe.wait_ge(s_ev, evacs(b, 2 * i + 1))
                atleast(pe, s_o, NQ * b + i)
                if i == 0:
                    pe.wait_ge(s_vp, 16 * (b + 1))
                for k in range(order[i] + 1):
                    for hl in range(2):
                        mm = pe.matmul(PS[HD * hl:HD * hl + HD, 7, 0:P], VP[:, k, HD * hl:HD * hl + HD],
                                       PT[hl][:, P * k:P * k + P], start=k == 0, stop=k == order[i])
                mm.then_inc(s_pv, 1)

            pe.wait_ge(s_bcon, 1)
            pe.wait_ge(s_pad2, 5)
            pe.wait_ge(s_knw, 32)
            pe.wait_ge(s_zc, PAIRS)
            steps(pe, att_step)

            for u in range(2 * KD):
                if u == 0:
                    pe.wait_ge(s_o, NQ * DB)
                    pe.wait_ge(s_wo[1], 16 * DB // 2)
                    pe.wait_ge(s_od, DB)
                    pe.wait_ge(s_os, DB)
                    pe.wait_ge(s_po, 16 * (DB - 1))
                if u >= 4:
                    pe.wait_ge(s_po, 16 * (DB - 1) + u - 3)
                pe.matmul(PS[:, 3 + u % 4, :], WOP[1][:, P * (u // 2):P * (u // 2) + P],
                          OP[1][:, 512 * (u % 2):512 * (u % 2) + 512], start=True, stop=True).then_inc(s_ou, 1)
            pe.wait_ge(s_oz, 1)
            for p in range(PAIRS):
                pe.wait_ge(s_wof, 16 * PAIRS)
                for c in range(2):
                    mm = pe.matmul(PS[0:RS, c, :], OS[:, p, :], WOF[p][:, 512 * c:512 * c + 512], start=p == 0,
                                   stop=p == PAIRS - 1)
            mm.then_inc(s_ys, 1)
            pe.wait_ge(s_yc, 1)
            for k in range(KD):
                mm = pe.transpose(PS[:, 2, RS * k:RS * k + RS], YS[:, P * k:P * k + P], FCON[0:RS, 0, 0:RS])
            mm.then_inc(s_yt, 1)
            pe.wait_ge(s_xl, 2 * KD + 1)
            ple(1, U_TAIL, (s_po, 16 * DB), (s_y, 1))


        @block.scalar
        def _(act):
            def hi(u, half_u, s, n=KD * P):
                act.wait_ge(s_raw[s], 16 * half_u + 16)
                atleast(act, s_unit, u - 1)
                act.activation(WH[s][:, 0:n], RAW[s][:, 0:n], ACT.Copy).then_inc(s_hi, 1)

            act.wait_ge(s_con, 32)
            for k in range(KD):
                act.wait_ge(s_xin[k], 16)
                atleast(act, s_st0, k - 1)
                act.activation(T0[k % 2][:], XIN[:, k, :], ACT.Square).then_inc(s_sq0, 1)
            hi(0, 0, 0)
            hi(1, 0, 1)
            act.wait_ge(s_st0, KD)
            for r, (a, b) in enumerate(RCH):
                i = act.activation(RSTD0[:, a:b], bank(1, r)[:, 0:b - a], ACT.Sqrt, scale=1.0 / D,
                                   bias=CST[:, C_EPS:C_EPS + 1])
            i.then_inc(s_sd0, 1)
            for k in range(KD):
                act.wait_ge(s_t0, k + 1)
                act.activation(HH[:, k, :], T0[k % 2][:], ACT.Copy).then_inc(s_hh, 1)

            def sigmoid_b(n, s, fills):
                act.wait_ge(s_est[s], 32 * fills)
                act.wait_ge(s_unit, 3 * n + 1)
                for r, (a, b) in enumerate(RCH):
                    for dst, x, y, dec in u_place(UX[s], r):
                        src = bank(s, r)[:, x:y]
                        i = act.activation(dst, rows3(src) if dec else src, ACT.Sigmoid)
                i.then_inc(s_sg, 1)

            act.wait_ge(s_pad, 2)
            sigmoid_b(0, 0, 1)
            hi(2, 1, 0)

            def products(n, s, qs):
                for q in qs:
                    if q == 0:
                        act.wait_ge(s_u, n + 1)
                    atleast(act, s_add, n * (NT - 1) + {0: -1, 1: 0, 2: 1}.get(q, q - 2))
                    j = NV + q
                    o = PROD[(s * NT + q) % 2]
                    act.activation(o[:, 0:SEQ], UX[s][:, j:j + SEQ], ACT.Copy, scale=CWT[s][:, j:j + 1])
                    act.activation(decode_rows(o), decode_window(UX[s], j), ACT.Copy,
                                   scale=CWT[s][:, j:j + 1]).then_inc(s_prod, 1)

            def chunk(n, s, i):
                last = isinstance(n, int) and n == NCH - 1
                hu = [3 * i + (3 * s + j) // 2 for j in (3, 4, 5)]
                hi(3 * n + 3, hu[0], (s + 3) % 2)
                products(n, s, range(0, 4))
                atleast(act, s_zst, 16 * n)
                act.wait_ge(s_unit, 3 * n + 3)
                for r, (a, b) in enumerate(RCH):
                    z = act.activation(ZS[:, a:b], bank(s, r)[:, 0:b - a], ACT.Silu)
                z.then_inc(s_zs, 1)
                act.wait_ge(s_zs, n + 1)
                act.dma_start(at(zT, n), ZS[:]).then_inc(s_zst, 16)
                hi(3 * n + 4, hu[1], (s + 4) % 2)
                products(n, s, range(4, 7))
                if not last:
                    sigmoid_b(n + 1, 1 - s, i + 1 + s)
                    hi(3 * n + 5, hu[2], (s + 5) % 2)
                products(n, s, range(7, NT))

            paired(act, NCH, chunk)
            act.wait_ge(s_mmu, 1)
            act.wait_ge(s_cst, 32 * NCH)
            act.wait_ge(s_zst, 16 * NCH)
            for r, (a, b) in enumerate(RCH):
                i = act.activation(MU[:, a:b], bank(0, r)[:, 0:b - a], ACT.Copy, scale=1.0 / EA)
            i.then_inc(s_mu, 1)
            for n in range(NCH):
                act.wait_ge(s_xc, n + 1)
                atleast(act, s_var, n // 2 - 1)
                act.activation(SQ1[n % 4][:], CC[:, n, :], ACT.Square).then_inc(s_sq1, 1)
            act.wait_ge(s_var, NCH // 2)
            for r, (a, b) in enumerate(RCH):
                i = act.activation(MU[:, a:b], bank(1, r)[:, 0:b - a], ACT.Sqrt, scale=1.0 / EA,
                                   bias=CST[:, C_EPS:C_EPS + 1])
            i.then_inc(s_sd1, 1)
            for n in range(NCH + 1):
                if n < NCH:
                    act.wait_ge(s_t1, n + 1)
                    atleast(act, s_ml, n - 2)
                    act.activation(Y1[n % 3][:], T1[n % 2][:], ACT.Silu, bias=CST[:, C_LB + n:C_LB + n + 1],
                                   scale=CST[:, C_LG + n:C_LG + n + 1]).then_inc(s_y1, 1)
                if n > 0:
                    act.wait_ge(s_m, n)
                    act.activation(MH[:, n - 1, :], Y1[(n - 1) % 3][:], ACT.Copy).then_inc(s_mh, 1)
            with act.Fori(0, 7) as i:
                hi(2 * i + 50, i + 25, 0)
                hi(2 * i + 51, i + 25, 1)
            def hi_next(u0, s, i, n=KD * P):
                hi(u0 + 2 * i + s + 1, i + (u0 + s + 1) // 2, (u0 + s + 1) % 2, n)

            def square2(m):
                act.wait_ge(s_x2, m + 1)
                act.wait_ge(s_ss2, m + 1)
                act.activation(SQ2[:], tile(X2, m), ACT.Square).then_inc(s_sq2, 1)

            def p_hi(l):
                act.wait_ge(s_prin, 16 * (l + 1))
                for j in range(2):
                    act.activation(PH[:, j, :], PR[:, j, :], ACT.Copy).then_inc(s_ph, 1)

            def ple(l, u0):
                def unit(m, s, i):
                    end = isinstance(m, int) and m == KD - 1
                    if not (end and l == 1):
                        hi_next(u0, s, i, KD * P if end else SLOT)
                    act.wait_ge(s_gate, KD * l + m + 1)
                    atleast(act, s_t2, KD * l + m)
                    for r, (a, b) in enumerate(RCH):
                        g = act.activation(SG[:, a:b], bank(0, r)[:, 0:b - a], ACT.Sigmoid)
                    g.then_inc(s_sgp, 1)
                    if l == 0 and not (isinstance(m, int) and m == 0):
                        square2(m - 1)
                paired(act, KD, unit)

            hi(U_PLE, U_PLE // 2, 0, SLOT)
            act.wait_ge(s_unit, U_PLE)
            act.dma_start(PR[:], pT[0]).then_inc(s_prin, 16)
            for k in range(KD):
                act.wait_ge(s_x1, k + 1)
                act.activation(XH[:, k, :], X2[:, k, :], ACT.Copy).then_inc(s_xh, 1)
                if k == 1:
                    p_hi(0)
            ple(0, U_PLE)
            square2(KD - 1)
            act.wait_ge(s_st2, 1)
            for r, (a, b) in enumerate(RCH):
                g = act.activation(RSTD2[:, a:b], bank(0, r)[:, 0:b - a], ACT.Sqrt, scale=1.0 / D,
                                   bias=CST[:, C_EPS:C_EPS + 1])
            g.then_inc(s_sd2, 1)

            def h_hi(base):
                for k in range(KD):
                    act.wait_ge(s_g, base + k + 1)
                    act.activation(GH[:, k, :], (KN, SQ3)[k % 2][:], ACT.Copy).then_inc(s_gh, 1)

            def copy_out(u, s):
                act.wait_ge(s_unit, u + 1)
                for r, (a, b) in enumerate(RCH):
                    g = act.activation(KC[s][:, a:b], bank(1, r)[:, 0:b - a], ACT.Copy)
                g.then_inc(s_kc, 1)

            def norm(p, keys=True):
                act.wait_ge(s_n, p + 1)
                atleast(act, s_kn, p)
                scale, eps = (1.0 / HD, C_EPS) if keys else (1.0, C_EPQ)
                for r, (a, b) in enumerate(RCH):
                    g = act.activation(RS3[:, a:b], bank(0, r)[:, 0:b - a], ACT.Sqrt, scale=scale,
                                       bias=CST[:, eps:eps + 1])
                g.then_inc(s_rs, 1)

            def square3(p, s, copies):
                atleast(act, s_n, p)
                act.wait_ge(s_kc, copies)
                act.activation(SQ3[:], KC[s][:], ACT.Square).then_inc(s_sq3, 1)

            def k_unit(m, s, i):
                hi_next(U_K, s, i)
                atleast(act, s_kn, m - 1)
                copy_out(U_K + m, s)
                if not (isinstance(m, int) and m == 0):
                    norm(m - 1)
                square3(m, s, m + 1)

            def v_unit(m, s, i):
                hi_next(U_V, s, i)
                if isinstance(m, int) and m < 2:
                    act.wait_ge(s_kn, PAIRS - 1 + m)
                else:
                    act.wait_ge(s_tr, m - 1)
                copy_out(U_V + m, s)
                if isinstance(m, int) and m == 0:
                    norm(PAIRS - 1)

            def q_unit(m, s, i):
                hi_next(U_Q, s, i)
                if isinstance(m, int) and m < 2:
                    act.wait_ge(s_tr, PAIRS - 1 + m)
                else:
                    act.wait_ge(s_kn, PAIRS + m - 1)
                copy_out(U_Q + m, s)
                if not (isinstance(m, int) and m == 0):
                    norm(PAIRS + m - 1, keys=False)
                square3(PAIRS + m, s, 2 * PAIRS + m + 1)

            def z_unit(m, s, i):
                if not (isinstance(m, int) and m == PAIRS - 1):
                    hi_next(U_Z, s, i)
                if isinstance(m, int) and m < 2:
                    act.wait_ge(s_kn, 2 * PAIRS - 1 + m)
                else:
                    act.wait_ge(s_gst[s], 16 * i)
                act.wait_ge(s_unit, U_Z + m + 1)
                for r, (a, b) in enumerate(RCH):
                    g = act.activation(KC[s][:, a:b], bank(1 - s, r)[:, 0:b - a], ACT.Silu)
                g.then_inc(s_zc, 1)
                if isinstance(m, int) and m == 0:
                    norm(2 * PAIRS - 1, keys=False)
                if isinstance(m, int) and m == 1:
                    act.wait_ge(s_f, 1)
                    act.activation(SQ3[0:H, :], SQ3[0:H, :], ACT.Exp).then_inc(s_fe, 1)

            h_hi(0)
            paired(act, PAIRS, k_unit)
            paired(act, PAIRS, v_unit)
            hi(U_Q, U_Q // 2, U_Q % 2)
            act.wait_ge(s_unit, U_F + 1)
            for r, (a, b) in enumerate(RCH):
                g = act.activation(FL[0:H, a:b], bank(1, r)[0:H, 0:b - a], ACT.Identity,
                                   bias=CST[0:H, C_FB:C_FB + 1])
            g.then_inc(s_fl, 1)
            h_hi(KD)
            paired(act, PAIRS, q_unit)
            paired(act, PAIRS, z_unit)

            def att_step(b, par, bh):
                real = not (isinstance(b, int) and b == DB)
                for t in range(16 if real else 1):
                    item, hl = order[t // 2], t % 2
                    if real and t > NG:
                        decode_keys_first(b, t)
                    if t == NG:
                        act.wait_ge(s_qn, b + 1)
                        act.activation(SC[:, PAST:PAST + RS], PS[:, 4, 0:RS], ACT.Copy).then_inc(s_sc, 1)
                    if started(b) or t > 0:
                        tp = (t - 1) % 16
                        bb = b if t else b - 1
                        n = P * (order[tp // 2] + 1)
                        atleast(act, s_pv, NQ * bb + tp // 2)
                        for c in range((n + 511) // 512):
                            a, e = 512 * c, min(n, 512 * c + 512)
                            act.wait_ge(s_trp, evacs(bb, tp, c))
                            act.activation(PT[tp % 2][:, a:e], PS[:, 5 + c, 0:e - a], ACT.Copy).then_inc(s_ev, 1)
                    if not real:
                        continue
                    n = P * (item + 1)
                    act.wait_ge(s_nm, 16 * b + t + 1)
                    atleast(act, s_trp, evacs(b, t - 2) if started(b) or t > 1 else 0)
                    act.activation(PP[hl][:, 0:n], PS[:, 2 * hl:2 * hl + 2, :].rearrange("p a n -> p (a n)")[:, 0:n],
                                   ACT.Exp, bias=NMX[hl][:], accum_out=SMP[hl][:]).then_inc(s_p, 1)
                    if t < NG:
                        if isinstance(b, int) and b == t == 0:
                            for s in range(2):
                                act.wait_ge(s_gst[s], 16 * PAIRS // 2)
                        act.wait_ge(s_dd, 16 * b + t + 1)
                        atleast(act, s_td, 9 * b)
                        act.activation(SC[:, 512 * t:512 * t + 512], PS[:, 4, :], ACT.Copy).then_inc(s_sc, 1)
                        continue
                    j = t - NG
                    if j == 0:
                        act.wait_ge(s_gm, b + 1)
                        atleast(act, s_rd, b)
                        dec_exp(NG)
                        dec_exp(0)
                        act.wait_ge(s_td, 9 * b + 1)
                        atleast(act, s_dd, 16 * b)
                        act.activation(PTN[:], PS[0:RS, 6, 0:P], ACT.Copy).then_inc(s_dv, 1)
                    if j < NG - 1:
                        dec_exp(j + 1)
                    if j == 0:
                        decode_keys_first(b, t)

            def decode_keys_first(b, t):
                j = t - NG
                act.wait_ge(s_td, 9 * b + j + 2)
                act.wait_ge(s_dd, 16 * b + t - 1)
                act.activation(PTD[j % 2][:], PS[:, 6, :].rearrange("p (k n) -> p k n", n=P),
                               ACT.Copy).then_inc(s_dv, 1)

            def dec_exp(c):
                a, e = (512 * c, 512 * c + 512) if c < NG else (PAST, PAST + RS)
                act.activation(SC[:, a:e], SC[:, a:e], ACT.Exp, bias=NGM[:],
                               accum_out=SMD[:, c:c + 1]).then_inc(s_ex, 1)

            steps(act, att_step)

            act.wait_ge(s_o, NQ * DB)
            act.dma_start(PR[:], pT[1]).then_inc(s_prin, 16)
            for k in range(KD):
                act.wait_ge(s_po, 16 * (DB - 1) + 2 * k + 2)
                act.activation(XH[:, k, 0:SEQ], X2[:, k, 0:SEQ], ACT.Copy).then_inc(s_xh, 1)
            p_hi(1)
            act.wait_ge(s_ou, 16 * DB)
            hi(U_TAIL, U_TAIL // 2, U_TAIL % 2, SLOT)
            act.wait_ge(s_ys, 1)
            act.activation(YS[:], PS[0:RS, 0:2, :].rearrange("p a n -> p (a n)"), ACT.Copy).then_inc(s_yc, 1)
            act.wait_ge(s_y, 1)
            act.activation(XH[:, :, SEQ:R], X2[:, :, SEQ:R], ACT.Copy).then_inc(s_xh, 1)
            ple(1, U_TAIL)


        @block.gpsimd
        def _(pool):
            def lo(u, s, n=KD * P):
                pool.wait_ge(s_hi, u + 1)
                pool.tensor_tensor(WL[s][:, 0:n], RAW[s][:, 0:n], WH[s][:, 0:n].bitcast(F32),
                                   ALU.subtract).then_inc(s_lo, 1)

            lo(0, 0)
            lo(1, 1)
            pool.wait_ge(s_h, KD)
            for s in range(2):
                pool.memset(UX[s][:, 0:HIST], 0.0).then_inc(s_pad, 1)
            pool.memset(CSUM[:], 0.0).then_inc(s_csum, 1)
            lo(2, 0)

            def adds(n, s, qs):
                for q in qs:
                    pool.wait_ge(s_prod, n * NT + q + 1)
                    if q == 1:
                        atleast(pool, s_c, n)
                        pool.tensor_tensor(ACC[:], PROD[(s * NT) % 2][:], PROD[(s * NT + 1) % 2][:],
                                           ALU.add).then_inc(s_add, 1)
                    else:
                        pool.wait_ge(s_add, n * (NT - 1) + q - 1)
                        pool.tensor_tensor(ACC[:], ACC[:], PROD[(s * NT + q) % 2][:], ALU.add).then_inc(s_add, 1)

            def csum(n):
                pool.wait_ge(s_c, n + 1)
                pool.wait_ge(s_csum, n + 1)
                src = tile(CC, n)
                pool.tensor_tensor(CSUM[:], CSUM[:], src, ALU.add).then_inc(s_csum, 1)

            def chunk(n, s, i):
                last = isinstance(n, int) and n == NCH - 1
                lo(3 * n + 3, (s + 3) % 2)
                if not (isinstance(n, int) and n == 0):
                    csum(n - 1)
                adds(n, s, range(1, 4))
                lo(3 * n + 4, (s + 4) % 2)
                adds(n, s, range(4, 7))
                if not last:
                    lo(3 * n + 5, (s + 5) % 2)
                adds(n, s, range(7, NT))

            paired(pool, NCH, chunk)
            csum(NCH - 1)
            for p in range(NCH // 2):
                pool.wait_ge(s_sq1, 2 * p + 2)
                a, b = SQ1[2 * (p % 2)], SQ1[2 * (p % 2) + 1]
                pool.tensor_tensor(a[:], a[:], b[:], ALU.add).then_inc(s_sqp, 1)
            for n in range(NCH):
                pool.wait_ge(s_mh, n + 1)
                pool.tensor_tensor(ML[:, n, :], Y1[n % 3][:], MH[:, n, :].bitcast(F32),
                                   ALU.subtract).then_inc(s_ml, 1)
            with pool.Fori(0, 7) as i:
                lo(2 * i + 50, 0)
                lo(2 * i + 51, 1)
            def lo_next(u0, s, i, n=KD * P):
                lo(u0 + 2 * i + s + 1, (u0 + s + 1) % 2, n)

            def add2(m):
                pool.wait_ge(s_sq2, m + 1)
                pool.wait_ge(s_ss2, m + 1)
                pool.tensor_tensor(SS2[:], SS2[:], SQ2[:], ALU.add).then_inc(s_ss2, 1)

            def p_lo(l):
                for j in range(2):
                    pool.wait_ge(s_ph, 2 * l + j + 1)
                    pool.tensor_tensor(PL[:, j, :], PR[:, j, :], PH[:, j, :].bitcast(F32),
                                       ALU.subtract).then_inc(s_pl, 1)

            def ple(l, u0):
                if l == 0:
                    pool.memset(SS2[:], 0.0).then_inc(s_ss2, 1)

                def unit(m, s, i):
                    end = isinstance(m, int) and m == KD - 1
                    if not (end and l == 1):
                        lo_next(u0, s, i, KD * P if end else SLOT)
                    if l == 0 and not (isinstance(m, int) and m == 0):
                        add2(m - 1)
                paired(pool, KD, unit)

            lo(U_PLE, 0, SLOT)
            p_lo(0)
            ple(0, U_PLE)
            add2(KD - 1)

            def store_kn(p, dst):
                pool.wait_ge(s_kn, p + 1)
                pool.dma_start(dst, KN[:]).then_inc(s_kst, 16)

            def store_v(m):
                cols = slice(m * P, m * P + P) if isinstance(m, int) else ds(m * P, P)
                pool.wait_ge(s_vr, m + 1)
                pool.dma_start(vR[0:SEQ, cols].rearrange("(c p) n -> p c n", p=P), VR[:, 0:SEQ // P, :]).then_inc(s_vst, 16)
                pool.dma_start(vR[SEQ:R, cols], VR[0:RS, SEQ // P, :]).then_inc(s_vst, 16)

            def store_g(m, s):
                pool.wait_ge(s_zc, m + 1)
                pool.dma_start(at(gT, m), KC[s][:]).then_inc(s_gst[s], 16)

            def store_past(c, s):
                cols = slice(c * 512, c * 512 + 512) if isinstance(c, int) else ds(c * 512, 512)
                pool.wait_ge(s_pb, c + 1)
                pool.dma_start(cPa[:, :, cols].rearrange("x h n -> h x n"), PB[s][:]).then_inc(s_pst[s], 16)

            def load_kq(b, par):
                pool.dma_start(KT[par][:], row(kT, b, 0, SEQ)).then_inc(s_q[par], 16)
                pool.dma_start(QT[par][:], row(qT, b, 0, SEQ)).then_inc(s_q[par], 16)
                hs = slice(2 * b, 2 * b + 2) if isinstance(b, int) else ds(2 * b, 2)
                for x in range(3):
                    pool.dma_start(CP[par][32 * x:32 * x + 2, :], cPr[x, hs, :]).then_inc(s_q[par], 16)

            def load_qc(b):
                cols = slice(SEQ + DS * b, SEQ + DS * b + DS) if isinstance(b, int) else ds(SEQ + DS * b, DS)
                for x in range(2):
                    for hl in range(2):
                        dst = QD[HD * hl:HD * hl + HD, :, :].rearrange("p (j x) n -> p j x n", x=2)[
                            :, :, x, 16 * x + DS * hl:16 * x + DS * hl + DS]
                        src = qT.rearrange("(j x) p n -> p j x n", x=2)[HD * hl:HD * hl + HD, :, x, cols]
                        pool.dma_start(dst, src).then_inc(s_qd, 16)
                hs = slice(H * b, H * b + H) if isinstance(b, int) else ds(H * b, H)
                for x in range(3):
                    pool.dma_start(CB[32 * x:32 * x + H, 0:PAST], cPa[x, hs, :]).then_inc(s_cb, 16)

            def row(t, i, a, e):
                return t[i, :, a:e] if isinstance(i, int) else t[ds(i, 1), :, a:e].rearrange("x a b -> (x a) b")

            def load_vz(b):
                cols = slice(P * b, P * b + P) if isinstance(b, int) else ds(P * b, P)
                pool.dma_start(VP[:], vR[0:SEQ, cols].rearrange("(c p) n -> p c n", p=P)).then_inc(s_vp, 16)
                pool.dma_start(ZP[:], row(gT, b, 0, SEQ)).then_inc(s_zp, 16)

            def pads():
                for s in range(2):
                    pool.wait_ge(s_pst[s], 64)
                for s in range(2):
                    pool.memset(CP[s][:], 0.0).then_inc(s_pad2, 1)
                pool.memset(QD[:], 0.0).then_inc(s_pad2, 1)
                pool.dma_start(BRAW[:], bcon[:, 0:B_BF]).then_inc(s_braw, 16)
                pool.dma_start(M4[:], bcon[:, B_M4:B_N]).then_inc(s_m4, 16)

            def pads_cb():
                pool.memset(CB[:], 0.0).then_inc(s_pad2, 1)

            def constants():
                pool.wait_ge(s_braw, 16)
                pool.tensor_copy(BCON[:], BRAW[:]).then_inc(s_bcon, 1)

            def new_kv():
                pool.wait_ge(s_vst, 32 * PAIRS)
                pool.dma_start(KNW[:], kT[:, :, SEQ:R].rearrange("a p n -> p a n")).then_inc(s_knw, 16)
                pool.dma_start(VNW[:], vR[SEQ:R, :]).then_inc(s_knw, 16)

            def queries():
                pool.wait_ge(s_kst, 32 * PAIRS)
                pool.wait_ge(s_bcon, 1)
                pool.wait_ge(s_pad2, 4)
                pool.dma_start(KT[0][:], kT[0, :, 0:SEQ]).then_inc(s_q[0], 16)
                pool.dma_start(QT[0][:], qT[0, :, 0:SEQ]).then_inc(s_q[0], 16)
                load_qc(0)

            def forget_out():
                pool.wait_ge(s_f, F_STEPS)
                pool.dma_start(lfT, FL[0:H, :]).then_inc(s_fst, 16)
                pool.dma_start(cPr.rearrange("x h n -> h x n"), FPB[:, :, 0:SEQ]).then_inc(s_fst, 16)
                pool.dma_start(cNw.rearrange("x h n -> h x n"), FPB[:, :, SEQ:R]).then_inc(s_fst, 16)

            def biases():
                pool.wait_ge(s_fst, 48)
                for x in range(3):
                    pool.dma_start(CP[0][32 * x:32 * x + 2, :], cPr[x, 0:2, :]).then_inc(s_q[0], 16)
                for x in range(3):
                    pool.dma_start(CB[32 * x:32 * x + H, PAST:PAST + RS], cNw[x]).then_inc(s_cb, 16)
                pool.wait_ge(s_gst[0], 64)
                load_vz(0)

            q_work = {0: pads, 1: pads_cb, 6: constants, 7: new_kv}
            z_work = {1: queries, 6: forget_out, 7: biases}

            def k_unit(m, s, i):
                lo_next(U_K, s, i)
                if not (isinstance(m, int) and m == 0):
                    store_kn(m - 1, at(kT, m - 1))

            def v_unit(m, s, i):
                lo_next(U_V, s, i)
                if isinstance(m, int) and m == 0:
                    store_kn(PAIRS - 1, kT[PAIRS - 1])
                else:
                    store_v(m - 1)
                    store_past(m - 1, 1 - s)

            def q_unit(m, s, i):
                lo_next(U_Q, s, i)
                if not (isinstance(m, int) and m == 0):
                    store_kn(PAIRS + m - 1, at(qT, m - 1))
                if isinstance(m, int) and m in q_work:
                    q_work[m]()

            def z_unit(m, s, i):
                if not (isinstance(m, int) and m == PAIRS - 1):
                    lo_next(U_Z, s, i)
                if isinstance(m, int) and m == 0:
                    store_kn(2 * PAIRS - 1, qT[PAIRS - 1])
                else:
                    store_g(m - 1, 1 - s)
                if isinstance(m, int) and m in z_work:
                    z_work[m]()

            paired(pool, PAIRS, k_unit)
            paired(pool, PAIRS, v_unit)
            lo(U_Q, U_Q % 2)
            store_v(PAIRS - 1)
            store_past(PAIRS - 1, 1)
            paired(pool, PAIRS, q_unit)
            paired(pool, PAIRS, z_unit)
            store_g(PAIRS - 1, 1)

            pool.wait_ge(s_unit, U_TAIL)
            for s in range(2):
                pool.wait_ge(s_gst[s], 16 * PAIRS // 2)
            pool.memset(SC[:, PAST + RS:], 0.0).then_inc(s_pad2, 1)

            def att_step(b, par, bh):
                if started(b):
                    pool.wait_ge(s_o, NQ * b)
                    load_vz(b)
                last = isinstance(b, int) and b == DB - 1
                if not last:
                    atleast(pool, s_s, 16 * b)
                    load_kq(b + 1, 1 - par)
                if started(b) and not (isinstance(b, int) and b == 1):
                    pool.wait_ge(s_ou, 16 * b - 16)
                pool.dma_start(WOP[par][:], at(wW, b)).then_inc(s_wo[par], 16)
                if not last:
                    pool.wait_ge(s_qn, b + 1)
                    load_qc(b + 1)

            paired(pool, DB, att_step)

            pool.wait_ge(s_qn, DB)
            pool.dma_start(ZSM[:], gT[:, :, SEQ:R].rearrange("a p n -> p a n")).then_inc(s_zsm, 16)
            pool.wait_ge(s_o, NQ * DB)
            pool.wait_ge(s_od, DB)
            for p in range(PAIRS):
                pool.dma_start(WOF[p][:], wW[p]).then_inc(s_wof, 16)
            p_lo(1)
            pool.wait_ge(s_ys, 1)
            lo(U_TAIL, U_TAIL % 2, SLOT)
            ple(1, U_TAIL)


        @block.vector
        def _(dve):
            dve.wait_ge(s_sd0, 1)
            dve.reciprocal(RSTD0[:], RSTD0[:]).then_inc(s_rc0, 1)
            dve.wait_ge(s_rc0, 1)
            for k in range(KD + 1):
                if k < KD:
                    atleast(dve, s_h, k - 1)
                    dve.scalar_tensor_tensor(out=T0[k % 2][:], in0=XIN[:, k, :], scalar=CST[:, C_AN + k:C_AN + k + 1],
                                             in1=RSTD0[:], op0=ALU.mult, op1=ALU.mult).then_inc(s_t0, 1)
                if k > 0:
                    dve.wait_ge(s_hh, k)
                    dve.tensor_tensor(HL[:, k - 1, :], T0[(k - 1) % 2][:], HH[:, k - 1, :].bitcast(F32),
                                      ALU.subtract).then_inc(s_h, 1)

            def chunk(n, s, i):
                dve.wait_ge(s_sg, n + 1)
                dve.wait_ge(s_unit, 3 * n + 2)
                for r, (a, b) in enumerate(RCH):
                    for dst, x, y, dec in u_place(UX[s], r):
                        src = bank(1 - s, r)[:, x:y]
                        i = dve.tensor_tensor(dst, rows3(src) if dec else src, dst, ALU.mult)
                i.then_inc(s_u, 1)
                dve.wait_ge(s_u, n + 1)
                w = CWT[s]
                for j in range(NV):
                    for part, (o, x) in enumerate(((CHAIN[:, 0:SEQ], UX[s][:, j:j + SEQ]),
                                                   (decode_rows(CHAIN), decode_window(UX[s], j)))):
                        if j == 0:
                            i = dve.tensor_scalar(o, x, w[:, 0:1], w[:, CW:CW + 1], ALU.mult, ALU.add)
                        else:
                            dve.wait_ge(s_tap, 2 * NV * n + 2 * (j - 1) + part + 1)
                            i = dve.scalar_tensor_tensor(out=o, in0=x, scalar=w[:, j:j + 1], in1=o,
                                                         op0=ALU.mult, op1=ALU.add)
                        i.then_inc(s_tap, 1)
                dve.wait_ge(s_tap, 2 * NV * (n + 1))
                dve.wait_ge(s_add, (n + 1) * (NT - 1))
                o = tile(CC, n)
                dve.tensor_tensor(o, CHAIN[:], ACC[:], ALU.add).then_inc(s_c, 1)

            paired(dve, NCH, chunk)
            dve.wait_ge(s_mu, 1)
            for n in range(NCH):
                dve.wait_ge(s_c, n + 1)
                dve.tensor_tensor(CC[:, n, :], CC[:, n, :], MU[:], ALU.subtract).then_inc(s_xc, 1)
            dve.wait_ge(s_sd1, 1)
            dve.reciprocal(MU[:], MU[:]).then_inc(s_rc1, 1)
            dve.wait_ge(s_rc1, 1)
            for n in range(NCH + 1):
                if n < NCH:
                    atleast(dve, s_y1, n - 1)
                    dve.wait_ge(s_xc, n + 1)
                    dve.tensor_tensor(T1[n % 2][:], CC[:, n, :], MU[:], ALU.mult).then_inc(s_t1, 1)
                if n > 0:
                    dve.wait_ge(s_y1, n)
                    dve.wait_ge(s_z1[(n - 1) % 2], 16 * ((n - 1) // 2 + 1))
                    dve.tensor_tensor(Y1[(n - 1) % 3][:], Y1[(n - 1) % 3][:], Z1[(n - 1) % 2][:],
                                      ALU.mult).then_inc(s_m, 1)
            dve.wait_ge(s_x1in, 16)

            def out0(m, st):
                dve.wait_ge(s_unit, U_OUT + 2 * m + 2)
                x = tile(X2, m)
                for r, (a, b) in enumerate(RCH):
                    i = dve.tensor_tensor(x[:, a:b], bank(st, r)[:, 0:b - a], x[:, a:b], ALU.add)
                i.then_inc(s_x1, 1)

            with dve.Fori(0, 4) as i:
                out0(2 * i, 0)
                out0(2 * i + 1, 1)
            def ple(l, u0):
                def unit(m, s, i):
                    dve.wait_ge(s_sgp, KD * l + m + 1)
                    atleast(dve, s_x2, KD * l + m)
                    dve.wait_ge(s_unit, u0 + m + 1)
                    for r, (a, b) in enumerate(RCH):
                        t = dve.tensor_tensor(T2[:, a:b], bank(1, r)[:, 0:b - a], SG[:, a:b], ALU.mult)
                    t.then_inc(s_t2, 1)
                    dve.wait_ge(s_t2, KD * l + m + 1)
                    x = tile(X2, m)
                    dve.tensor_tensor(x, x, T2[:], ALU.add).then_inc(s_x2, 1)
                paired(dve, KD, unit)

            for k in range(KD):
                dve.wait_ge(s_xh, k + 1)
                dve.tensor_tensor(XL[:, k, :], X2[:, k, :], XH[:, k, :].bitcast(F32), ALU.subtract).then_inc(s_xl, 1)
            ple(0, U_PLE)
            dve.wait_ge(s_sd2, 1)
            dve.reciprocal(RSTD2[:], RSTD2[:]).then_inc(s_rc2, 1)
            dve.wait_ge(s_rc2, 1)

            def h_split(base, gain):
                for k in range(KD + 1):
                    if k < KD:
                        atleast(dve, s_gl, base + k - 1 if k > 1 or base else 0)
                        dve.scalar_tensor_tensor(out=(KN, SQ3)[k % 2][:], in0=X2[:, k, :],
                                                 scalar=CST[:, gain + k:gain + k + 1],
                                                 in1=RSTD2[:], op0=ALU.mult, op1=ALU.mult).then_inc(s_g, 1)
                    if k > 0:
                        dve.wait_ge(s_gh, base + k)
                        dve.tensor_tensor(GL[:, k - 1, :], (KN, SQ3)[(k - 1) % 2][:], GH[:, k - 1, :].bitcast(F32),
                                          ALU.subtract).then_inc(s_gl, 1)

            def norm(p, s, gain):
                dve.wait_ge(s_rs, p + 1)
                dve.reciprocal(RS3[:], RS3[:]).then_inc(s_rc, 1)
                dve.wait_ge(s_rc, p + 1)
                atleast(dve, s_kst, 16 * p)
                dve.scalar_tensor_tensor(out=KN[:], in0=KC[s][:], scalar=CST[:, gain:gain + 1], in1=RS3[:],
                                         op0=ALU.mult, op1=ALU.mult).then_inc(s_kn, 1)

            def rows_first(m):
                dve.wait_ge(s_tr, m + 1)
                if isinstance(m, int) and m == 0:
                    dve.wait_ge(s_kn, PAIRS)
                else:
                    dve.wait_ge(s_vst, 32 * m)
                for c in range(2):
                    dve.tensor_copy(VR[:, 4 * c:4 * c + 4, :], PS[:, c, :].rearrange("p (c n) -> p c n", n=P))
                dve.tensor_copy(VR[0:RS, SEQ // P, :], PS[0:RS, 2, 0:P]).then_inc(s_vr, 1)

            def k_unit(m, s, i):
                if not (isinstance(m, int) and m == 0):
                    norm(m - 1, 1 - s, C_K2)

            def past_sums():
                dve.memset(CUM[:, 0:1], 0.0).then_inc(s_cum, 1)
                dve.wait_ge(s_lfp, 16)
                dve.wait_ge(s_cum, 1)
                dve.tensor_tensor_scan(CUM[:, 1:], LFP[:], LFP[:], CUM[:, 0:1], ALU.add, ALU.bypass).then_inc(s_cum, 1)
                dve.wait_ge(s_cum, 2)
                dve.tensor_scalar(VRES[:], CUM[:, 1:], CUM[:, PAST:], -1.0, ALU.subtract, ALU.mult).then_inc(s_vres, 1)

            def past_parts(c, s, i):
                v = VRES[:, c * 512:(c + 1) * 512] if isinstance(c, int) else VRES[:, ds(c * 512, 512)]
                if not (isinstance(c, int) and c < 2):
                    dve.wait_ge(s_pst[s], 16 * i)
                for x in range(3):
                    dve.wait_ge(s_vres, 1 + 4 * c + 2 * x)
                    dve.tensor_scalar(PB[s][:, x, :], v, 1.0, None, ALU.mult).then_inc(s_pb if x == 2 else s_vres, 1)
                    if x < 2:
                        dve.wait_ge(s_vres, 2 + 4 * c + 2 * x)
                        dve.tensor_tensor(v, v, PB[s][:, x, :], ALU.subtract).then_inc(s_vres, 1)

            def v_unit(m, s, i):
                if isinstance(m, int) and m == 0:
                    norm(PAIRS - 1, 1, C_K2)
                    past_sums()
                else:
                    rows_first(m - 1)
                    past_parts(m - 1, 1 - s, i - (1 - s))

            def q_unit(m, s, i):
                if not (isinstance(m, int) and m == 0):
                    norm(PAIRS + m - 1, 1 - s, C_Q2)

            dve.wait_ge(s_unit, U_K)
            h_split(0, C_KN)
            paired(dve, PAIRS, k_unit)
            paired(dve, PAIRS, v_unit)
            rows_first(PAIRS - 1)
            past_parts(PAIRS - 1, 1, PAIRS // 2 - 1)
            dve.wait_ge(s_unit, U_F + 1)
            dve.wait_ge(s_kst, 16 * PAIRS)
            dve.wait_ge(s_vst, 32 * PAIRS)
            h_split(KD, C_BN)
            paired(dve, PAIRS, q_unit)
            norm(2 * PAIRS - 1, 1, C_Q2)
            F, E, S, A = FL[0:H, :], SQ3[0:H, :], RS3[0:H, :], KN[0:H, :]
            dve.wait_ge(s_fl, 1)
            dve.wait_ge(s_n, 2 * PAIRS)
            dve.scalar_tensor_tensor(out=E, in0=F, scalar=-1.0, in1=F, op0=ALU.mult, op1=ALU.min).then_inc(s_f, 1)
            dve.wait_ge(s_fe, 1)
            dve.tensor_scalar(S, E, 1.0, 2.0, ALU.mult, ALU.add).then_inc(s_f, 1)
            dve.wait_ge(s_f, 2)
            dve.reciprocal(S, S).then_inc(s_f, 1)
            dve.wait_ge(s_f, 3)
            dve.tensor_tensor(E, E, S, ALU.mult).then_inc(s_f, 1)
            dve.wait_ge(s_f, 4)
            dve.tensor_tensor(S, E, E, ALU.mult).then_inc(s_f, 1)
            dve.wait_ge(s_f, 5)
            dve.wait_ge(s_kst, 32 * PAIRS)
            dve.tensor_scalar(A, S, 1.0 / 15, 0.0, ALU.mult, ALU.add).then_inc(s_f, 1)
            for j, odd in enumerate((13, 11, 9, 7, 5, 3)):
                dve.wait_ge(s_f, 6 + j)
                dve.scalar_tensor_tensor(out=A, in0=A, scalar=1.0 / odd, in1=S, op0=ALU.add,
                                         op1=ALU.mult).then_inc(s_f, 1)
            dve.wait_ge(s_f, 12)
            dve.scalar_tensor_tensor(out=A, in0=A, scalar=1.0, in1=E, op0=ALU.add, op1=ALU.mult).then_inc(s_f, 1)
            dve.wait_ge(s_f, 13)
            dve.tensor_scalar(S, F, 0.0, 1.0, ALU.min, ALU.mult).then_inc(s_f, 1)
            dve.wait_ge(s_f, 14)
            dve.scalar_tensor_tensor(out=F, in0=A, scalar=-2.0, in1=S, op0=ALU.mult, op1=ALU.add).then_inc(s_f, 1)
            dve.wait_ge(s_f, 15)
            dve.memset(RSTD2[0:H, 0:1], 0.0).then_inc(s_zero, 1)
            dve.wait_ge(s_zero, 1)
            dve.tensor_scalar(E, F, -1.0, 0.0, ALU.mult, ALU.add).then_inc(s_f, 1)
            dve.wait_ge(s_f, 16)
            for a, b in [(0, SEQ)] + [(a, a + DS) for a in range(SEQ, R, DS)]:
                t = dve.tensor_tensor_scan(A[:, a:b], E[:, a:b], E[:, a:b], RSTD2[0:H, 0:1], ALU.add, ALU.bypass)
            t.then_inc(s_f, 1)
            for x in range(3):
                dve.wait_ge(s_f, 17 + 2 * x)
                dve.tensor_copy(FPB[:, x, :], A).then_inc(s_f, 1)
                if x < 2:
                    dve.wait_ge(s_f, 18 + 2 * x)
                    dve.tensor_tensor(A, A, FPB[:, x, :], ALU.subtract).then_inc(s_f, 1)

            def att_step(b, par, bh):
                real = not (isinstance(b, int) and b == DB)
                for t in range(16 if real else 1):
                    item, hl = order[t // 2], t % 2
                    n = P * (item + 1)
                    if real:
                        atleast(dve, s_nm, 16 * b + t - 1)
                        dve.wait_ge(s_s, 16 * b + t + 1)
                        dve.tensor_reduce(MXP[hl][:], PS[:, 2 * hl:2 * hl + 2, :].rearrange("p a n -> p (a n)")[:, 0:n],
                                          AX_X, ALU.max).then_inc(s_mx, 1)
                        dve.wait_ge(s_mx, 16 * b + t + 1)
                        atleast(dve, s_p, 16 * b + t - 1)
                        dve.tensor_scalar(NMX[hl][:], MXP[hl][:], -1.0, 0.0, ALU.mult, ALU.add).then_inc(s_nm, 1)
                    if t == 0 and started(b):
                        dve.wait_ge(s_ex, 9 * b)
                        dve.tensor_reduce(RID[:], SMD[:], AX_X, ALU.add).then_inc(s_rd, 1)
                        dve.wait_ge(s_rd, b)
                        dve.reciprocal(RID[:], RID[:]).then_inc(s_ridn, 1)
                        dve.wait_ge(s_ridn, b)
                        dve.wait_ge(s_dd, 16 * b)
                        dve.scalar_tensor_tensor(out=OD[:], in0=PS[:, 4, 0:4 * HD], scalar=RID[:], in1=M4[:],
                                                 op0=ALU.mult, op1=ALU.mult).then_inc(s_od, 1)
                        dve.wait_ge(s_od, b)
                        atleast(dve, s_to, b - 1)
                        dve.tensor_reduce(OE[:, 0:HD], OD[:].rearrange("p (g d) -> p d g", d=HD), AX_X,
                                          ALU.add).then_inc(s_oe, 1)
                        dve.wait_ge(s_oe, b)
                        dve.tensor_copy(OE[:, HD:2 * HD], OE[:, 0:HD]).then_inc(s_oe2, 1)
                    if t == NG and real:
                        dve.wait_ge(s_sc, 9 * b + NG + 1)
                        dve.tensor_reduce(MXD[:, NG:NG + 1], SC[:, PAST:PAST + RS], AX_X, ALU.max).then_inc(s_dmx, 1)
                        dve.wait_ge(s_dmx, 9 * (b + 1))
                        dve.tensor_reduce(GMD[:], MXD[:], AX_X, ALU.max).then_inc(s_gmx, 1)
                        dve.wait_ge(s_gmx, b + 1)
                        atleast(dve, s_ex, 9 * b)
                        dve.tensor_scalar(NGM[:], GMD[:], -1.0, 0.0, ALU.mult, ALU.add).then_inc(s_gm, 1)
                    if real:
                        dve.wait_ge(s_p, 16 * b + t + 1)
                        atleast(dve, s_pn, 16 * b + t - 1)
                        dve.reciprocal(RIP[hl][:], SMP[hl][:]).then_inc(s_ri, 1)
                        dve.wait_ge(s_ri, 16 * b + t + 1)
                        dve.tensor_scalar(PP[hl][:, 0:n], PP[hl][:, 0:n], RIP[hl][:], None, ALU.mult).then_inc(s_pn, 1)
                    if t == 0 and started(b):
                        prompt_o(b - 1, NQ - 1, 1 - par)
                        dve.wait_ge(s_to, b)
                        cols = slice(DS * b - DS, DS * b) if isinstance(b, int) else ds(DS * b - DS, DS)
                        for x in range(2):
                            src = PS[HD * x:HD * x + HD, 6, 0:P].rearrange("p (j x q) -> p j x q", x=2, q=DS)[:, :, x, :]
                            o = dve.tensor_copy(OS[HD * x:HD * x + HD, :, cols], src)
                        o.then_inc(s_os, 1)
                    if started(b) and real:
                        half, mo = t // 8, t % 8
                        dve.wait_ge(s_ou, 16 * b - 16 + t + 1)
                        atleast(dve, s_po, 16 * b - 32 + t + 1 if not (isinstance(b, int) and b == 1) else 0)
                        x = X2[:, mo, 512 * half:512 * half + 512]
                        dve.tensor_tensor(x, PS[:, 5, :], x, ALU.add).then_inc(s_po, 1)
                    if not real:
                        continue
                    if t >= 2 and hl == 0:
                        prompt_o(b, t // 2 - 1, par)
                    if t < NG:
                        dve.wait_ge(s_sc, 9 * b + t + 1)
                        atleast(dve, s_gmx, b)
                        dve.tensor_reduce(MXD[:, t:t + 1], SC[:, 512 * t:512 * t + 512], AX_X, ALU.max).then_inc(s_dmx, 1)

            def prompt_o(b, i, par):
                dve.wait_ge(s_pv, NQ * b + i + 1)
                if i == 0:
                    dve.wait_ge(s_zp, 16 * (b + 1))
                    if not (isinstance(b, int) and b < 2):
                        dve.wait_ge(s_ou, 16 * b - 16)
                c = slice(P * order[i], P * order[i] + P)
                dve.tensor_tensor(OP[par][:, c], PS[:, 7, 0:P], ZP[:, c], ALU.mult).then_inc(s_o, 1)

            dve.wait_ge(s_m4, 16)
            steps(dve, att_step)

            dve.wait_ge(s_zsm, 16)
            dve.wait_ge(s_os, DB)
            dve.tensor_tensor(OS[:], OS[:], ZSM[:], ALU.mult).then_inc(s_oz, 1)
            for k in range(KD + 1):
                if k < KD:
                    for half in range(2):
                        u = 2 * k + half
                        dve.wait_ge(s_ou, 16 * (DB - 1) + u + 1)
                        dve.wait_ge(s_po, 16 * (DB - 1))
                        x = X2[:, k, 512 * half:512 * half + 512]
                        dve.tensor_tensor(x, PS[:, 3 + u % 4, :], x, ALU.add).then_inc(s_po, 1)
                if k > 0:
                    dve.wait_ge(s_xh, KD + k)
                    dve.tensor_tensor(XL[:, k - 1, 0:SEQ], X2[:, k - 1, 0:SEQ], XH[:, k - 1, 0:SEQ].bitcast(F32),
                                      ALU.subtract).then_inc(s_xl, 1)
            dve.wait_ge(s_yt, 1)
            x = X2[:, :, SEQ:R]
            dve.tensor_tensor(x, x, PS[:, 2, :].rearrange("p (k n) -> p k n", n=RS), ALU.add).then_inc(s_y, 1)
            dve.wait_ge(s_xh, 2 * KD + 1)
            dve.tensor_tensor(XL[:, :, SEQ:R], x, XH[:, :, SEQ:R].bitcast(F32), ALU.subtract).then_inc(s_xl, 1)
            ple(1, U_TAIL)



def layout(x_prompt, x_sample, state_conv, cache_k, cache_v, cache_logf, page_table, p_prompt, p_sample,
           a_norm, a_w_in, a_conv_w, a_conv_b, a_ln_g, a_ln_b, a_w_out, kv_norm, kv_w, kv_k_norm, kv_f_bias,
           b_norm, b_w_q, b_q_norm, b_w_out, ple_w, ple_gate_w):
    import numpy as np

    def features_first(a):
        return a.T.reshape(a.shape[1] // P, P, a.shape[0]).transpose(1, 0, 2)

    def units(w):
        k, n = w.shape
        return w.reshape(k // P, P, n // P, P).transpose(2, 1, 0, 3).reshape(n // P, P, k)

    def columns(v):
        return v.reshape(-1, P).T

    rows = np.concatenate([x_prompt[0], x_sample.reshape(RS, D)], 0)
    prow = [np.concatenate([p_prompt[l, 0], p_sample[l].reshape(RS, PLE)], 0) for l in range(2)]
    conv = units(a_w_in[0]).reshape(3, NCH, P, D)
    conv = np.stack([conv[1], conv[0], conv[2]], 1).reshape(3 * NCH, P, D)
    wo = a_w_out[0].reshape(2, D, D)
    wo = np.stack([units(wo[0]), units(wo[1])], 1).reshape(2 * KD, P, D)
    ple = np.stack([np.concatenate([units(ple_gate_w[l]), units(ple_w[l])], 2) for l in range(2)])
    fl = np.zeros((D, P), np.float32)
    fl[:, :H] = kv_w[:, 2 * D:]
    kvq = np.concatenate([units(kv_w[:, :2 * D]), units(fl), units(b_w_q[0])], 0)
    taps = np.concatenate([a_conv_w[0], a_conv_b], 0)
    taps = taps.T.reshape(NCH, P, CW + 1)
    state = np.zeros((EA, DB, SW), np.float32)
    state[:, :, :HIST] = state_conv[0].transpose(2, 0, 1)
    fb = np.zeros((P, 1), np.float32)
    fb[:H, 0] = kv_f_bias
    twice = lambda g: np.concatenate([g, g])[:, None]
    eps = np.full((P, 1), EPS, np.float32)
    cst = np.concatenate([columns(a_norm[0]), columns(kv_norm), columns(b_norm[0]), columns(a_ln_g[0]),
                          columns(a_ln_b[0]), twice(kv_k_norm), twice(b_q_norm[0]), fb, eps, HD * eps], 1)
    ident = np.eye(P, dtype=np.float32)
    bones = np.kron(np.eye(2), np.ones((HD, HD))).astype(np.float32)
    fcon = np.stack([ident, np.ones((P, P), np.float32), bones], 1)
    bcon = np.zeros((P, B_N), np.float32)
    bcon[:, B_ID:B_ID + P] = ident
    i = np.arange(P)
    bcon[:, B_MD:B_MD + P] = np.where(i[None, :] > i[:, None], -1e30, 0)
    hq = np.arange(P)
    for part in range(3):
        bcon[32 * part + hq // DS, B_SD + hq] = 1
        for hl in range(2):
            bcon[32 * part + hl, B_SP + P * hl:B_SP + P * hl + P] = 1
    for b in range(DB):
        key = np.arange(RS)
        seen = (key[None, :] // DS == b) & (key[None, :] % DS <= hq[:, None] % DS)
        bcon[:, B_MN + RS * b:B_MN + RS * b + RS] = np.where(seen, 0, -1e30)
    for g in range(4):
        bcon[:, B_M4 + HD * g:B_M4 + HD * g + HD] = (hq[:, None] // DS % 4 == g)
    c = np.ascontiguousarray
    return {
        "xT": c(features_first(rows)), "pT": c(np.stack([features_first(p) for p in prow])),
        "wA": c(conv), "wO": c(wo), "wP": c(ple), "wB": c(kvq), "wW": c(b_w_out[0].reshape(PAIRS, P, D)),
        "cw": c(taps), "est": c(state.reshape(NCH, P, DB * SW)), "cst": c(cst), "fcon": c(fcon), "bcon": bcon,
        "ck": c(cache_k.reshape(-1, PAGE, PAIRS, P).transpose(0, 3, 2, 1)).reshape(-1, P, D),
        "cv": c(cache_v.reshape(-1, PAGE, D)), "clf": c(cache_logf.transpose(0, 2, 1)),
        "ptab": c(page_table.reshape(1, DB * NPG)),
    }


_OUTS = [("yT", (P, KD, R)), ("cpT", (NCH, P, HIST)), ("csT", (NCH, P, DB * SW)), ("kT", (PAIRS, P, R)),
         ("vR", (R, D)), ("lfT", (H, R))]


def kernel(**inputs):
    import numpy as np
    import concourse.bacc as bacc
    from concourse.bass_utils import run_bass_kernel_spmd as run

    arrays = layout(**{k: np.asarray(v) for k, v in inputs.items()})
    nc = bacc.Bacc("TRN2", target_bir_lowering=False, num_devices=1)
    args = [nc.dram_tensor(n, a.shape, mybir.dt.from_np(a.dtype), kind="ExternalInput").ap()
            for n, a in arrays.items()]
    args += [nc.dram_tensor(n, s, F32, kind="ExternalOutput").ap() for n, s in _OUTS]
    build(nc, *args)
    got = run(nc, [arrays], core_ids=[0]).results[0]
    y = got["yT"].transpose(2, 1, 0).reshape(R, D)
    conv_p = got["cpT"].transpose(2, 0, 1).reshape(1, 1, HIST, EA)
    conv_s = got["csT"].reshape(NCH, P, DB, SW)[..., DS:].transpose(2, 3, 0, 1).reshape(1, DB, HIST, EA)
    k = got["kT"].transpose(2, 0, 1).reshape(R, H, HD)
    v = got["vR"].reshape(R, H, HD)
    lf = got["lfT"].T
    c = np.ascontiguousarray
    return (c(y[:SEQ]).reshape(1, SEQ, D), c(y[SEQ:]).reshape(DB, DS, D), c(conv_p),
            c(k[:SEQ])[None], c(v[:SEQ])[None], c(lf[:SEQ])[None], c(conv_s),
            c(k[SEQ:]).reshape(DB, DS, H, HD), c(v[SEQ:]).reshape(DB, DS, H, HD), c(lf[SEQ:]).reshape(DB, DS, H))
```
